# Optimizing a Trainium2 kernel written in Bass

```python
import math
import jax, jax.numpy as jnp
from jax import lax
import numpy as np

D_MODEL = 1024
BATCH = 1
SEQ = 128
DEPTH = 1
DEC_BATCH = 1
DEC_SEQ = 128
PAST_LEN = 128

GRID_W = 64
D_S5 = 768
S5_H = 16
N_S5_GROUPS = D_S5 // S5_H
S5_STATE = 64
D_FNET = D_MODEL - D_S5
N_FNET_GROUPS = 4
FNET_GW = D_FNET // N_FNET_GROUPS
N_EXPERTS = 32
TOP_K = 4
D_FF = D_MODEL
SWIGLU_LIMIT = 7.0
SWIGLU_ALPHA = 1.702
RMS_EPS = 1e-6
DT_MIN = 1e-3
DT_MAX = 1e-1
POS_TEMP = 10000.0

kernel_name = 'hymba_s5_fnet_moe_diffusion_step'

def rms_norm(x, g):
    xf = x.astype(jnp.float32)
    y = xf * lax.rsqrt(jnp.mean(xf * xf, axis=-1, keepdims=True) + RMS_EPS)
    return (y * g.astype(jnp.float32)).astype(x.dtype)

def grid_pos_embed(n_tokens, dim, dtype):
    rows = n_tokens // GRID_W
    t = jnp.arange(rows * GRID_W)
    r = (t // GRID_W).astype(jnp.float32)
    col = (t % GRID_W).astype(jnp.float32)
    q = dim // 4
    omega = 1.0 / POS_TEMP ** (jnp.arange(q, dtype=jnp.float32) / q)

    def emb(p):
        a = p[:, None] * omega[None, :]
        return jnp.concatenate([jnp.sin(a), jnp.cos(a)], axis=-1)

    return jnp.concatenate([emb(r), emb(col)], axis=-1).astype(dtype)

def cmul(ar, ai, br, bi):
    return ar * br - ai * bi, ar * bi + ai * br

def scan_combine(e1, e2):
    a1r, a1i, b1r, b1i = e1
    a2r, a2i, b2r, b2i = e2
    ar, ai = cmul(a2r, a2i, a1r, a1i)
    br, bi = cmul(a2r, a2i, b1r, b1i)
    return ar, ai, br + b2r, bi + b2i

def s5_mixer(u, init_re, init_im, lam_re, lam_im, log_dt, b_re, b_im, c_re, c_im, d_skip, w_glu):
    bsz, L, _ = u.shape
    uf = u.astype(jnp.float32)
    ug = uf.reshape(bsz, L, N_S5_GROUPS, S5_H)
    y = d_skip.astype(jnp.float32) * uf
    finals_re = []
    finals_im = []
    for d in range(2):
        reverse = d == 1
        dt = jnp.exp(log_dt[d].astype(jnp.float32))[:, None]
        a_re = jnp.minimum(lam_re[d].astype(jnp.float32), -1e-4)
        a_im = lam_im[d].astype(jnp.float32)
        mag = jnp.exp(a_re * dt)
        ab_re = mag * jnp.cos(a_im * dt)
        ab_im = mag * jnp.sin(a_im * dt)
        den = a_re * a_re + a_im * a_im
        nr = ab_re - 1.0
        f_re = (nr * a_re + ab_im * a_im) / den
        f_im = (ab_im * a_re - nr * a_im) / den
        bb_re, bb_im = cmul(f_re[..., None], f_im[..., None],
                            b_re[d].astype(jnp.float32), b_im[d].astype(jnp.float32))
        bu_re = jnp.einsum('blgh,gph->blgp', ug, bb_re)
        bu_im = jnp.einsum('blgh,gph->blgp', ug, bb_im)
        s0r, s0i = cmul(ab_re, ab_im, init_re[:, d].astype(jnp.float32), init_im[:, d].astype(jnp.float32))
        first = L - 1 if reverse else 0
        last = 0 if reverse else L - 1
        bu_re = bu_re.at[:, first].add(s0r)
        bu_im = bu_im.at[:, first].add(s0i)
        a_br = jnp.broadcast_to(ab_re, bu_re.shape)
        a_bi = jnp.broadcast_to(ab_im, bu_im.shape)
        _, _, s_re, s_im = lax.associative_scan(scan_combine, (a_br, a_bi, bu_re, bu_im),
                                                reverse=reverse, axis=1)
        finals_re.append(s_re[:, last])
        finals_im.append(s_im[:, last])
        yd = (jnp.einsum('blgp,ghp->blgh', s_re, c_re[d].astype(jnp.float32))
              - jnp.einsum('blgp,ghp->blgh', s_im, c_im[d].astype(jnp.float32)))
        y = y + yd.reshape(bsz, L, D_S5)
    z = jax.nn.gelu(y)
    out = z * jax.nn.sigmoid(z @ w_glu.astype(jnp.float32))
    return out.astype(u.dtype), jnp.stack(finals_re, axis=1), jnp.stack(finals_im, axis=1)

def fourier_mixer(u, w_fnet):
    bsz, L, _ = u.shape
    ug = u.astype(jnp.float32).reshape(bsz, L, N_FNET_GROUPS, FNET_GW)
    f = jnp.fft.fft2(ug, axes=(1, 3), norm='ortho').real
    out = jnp.einsum('blgc,gce->blge', f, w_fnet.astype(jnp.float32)).reshape(bsz, L, D_FNET)
    return out.astype(u.dtype)

def moe(h, w_router, b_router, w_gate, b_gate, w_up, b_up, w_down, b_down):
    bsz, L, D = h.shape
    t = h.reshape(bsz * L, D)
    logits = t.astype(jnp.float32) @ w_router.astype(jnp.float32) + b_router.astype(jnp.float32)
    top_v, top_i = lax.top_k(logits, TOP_K)
    top_w = jax.nn.softmax(top_v, axis=-1)
    comb = jnp.sum(jax.nn.one_hot(top_i, N_EXPERTS, dtype=jnp.float32) * top_w[..., None], axis=1)
    comb = comb.astype(h.dtype)
    gate = jnp.einsum('td,edf->tef', t, w_gate) + b_gate
    up = jnp.einsum('td,edf->tef', t, w_up) + b_up
    gate = jnp.minimum(gate, SWIGLU_LIMIT)
    up = jnp.clip(up, -SWIGLU_LIMIT, SWIGLU_LIMIT)
    act = (up + 1.0) * gate * jax.nn.sigmoid(SWIGLU_ALPHA * gate) * comb[..., None]
    out = jnp.einsum('tef,efd->td', act, w_down) + comb @ b_down
    return out.reshape(bsz, L, D)

def trunk_layer(x, mod, s_init_re, s_init_im, p):
    shift1, scale1, gate1, shift2, scale2, gate2 = jnp.split(mod, 6, axis=-1)
    h = rms_norm(x, p['norm1_g']) * (1.0 + scale1) + shift1
    proj = h @ p['w_in']
    u_s5 = proj[..., :D_S5]
    u_f = proj[..., D_S5:]
    y_s5, fin_re, fin_im = s5_mixer(u_s5, s_init_re, s_init_im, p['lam_re'], p['lam_im'], p['log_dt'],
                                    p['b_re'], p['b_im'], p['c_re'], p['c_im'], p['d_skip'], p['w_glu'])
    y_f = fourier_mixer(u_f, p['w_fnet'])
    x = x + gate1 * (jnp.concatenate([y_s5, y_f], axis=-1) @ p['w_out'])
    h2 = rms_norm(x, p['norm2_g']) * (1.0 + scale2) + shift2
    x = x + gate2 * moe(h2, p['w_router'], p['b_router'], p['w_gate'], p['b_gate'],
                        p['w_up'], p['b_up'], p['w_down'], p['b_down'])
    return x, fin_re, fin_im

def setup_inputs(seed: int = 0) -> dict:
    key = jax.random.key(seed)
    ks = jax.random.split(key, 32)
    f32 = jnp.float32

    def nrm(k, shape, scale):
        return scale * jax.random.normal(k, shape, f32)

    G, P, H, E, D = N_S5_GROUPS, S5_STATE, S5_H, N_EXPERTS, D_MODEL
    lam_im = jnp.broadcast_to(jnp.pi * jnp.arange(P, dtype=f32), (DEPTH, 2, G, P)) + nrm(ks[7], (DEPTH, 2, G, P), 0.01)
    return {
        'x_prompt': nrm(ks[0], (BATCH, SEQ, D), 1.0),
        'x_sample': nrm(ks[1], (DEC_BATCH, DEC_SEQ, D), 1.0),
        'c': nrm(ks[2], (DEC_BATCH, D), 1.0),
        'state_s5_re': nrm(ks[3], (DEC_BATCH, DEPTH, 2, G, P), 0.3),
        'state_s5_im': nrm(ks[4], (DEC_BATCH, DEPTH, 2, G, P), 0.3),
        'c_ctx': nrm(ks[5], (D,), 1.0),
        'w_ada': nrm(ks[6], (DEPTH, D, 6 * D), D ** -0.5),
        'b_ada': nrm(ks[8], (DEPTH, 6 * D), 0.01),
        'norm1_g': 1.0 + nrm(ks[9], (DEPTH, D), 0.02),
        'w_in': nrm(ks[10], (DEPTH, D, D), D ** -0.5),
        's5_lam_re': -0.5 + nrm(ks[11], (DEPTH, 2, G, P), 0.01),
        's5_lam_im': lam_im,
        's5_log_dt': jax.random.uniform(ks[12], (DEPTH, 2, G), f32, math.log(DT_MIN), math.log(DT_MAX)),
        's5_b_re': nrm(ks[13], (DEPTH, 2, G, P, H), (2 * H) ** -0.5),
        's5_b_im': nrm(ks[14], (DEPTH, 2, G, P, H), (2 * H) ** -0.5),
        's5_c_re': nrm(ks[15], (DEPTH, 2, G, H, P), (2 * P) ** -0.5),
        's5_c_im': nrm(ks[16], (DEPTH, 2, G, H, P), (2 * P) ** -0.5),
        's5_d': nrm(ks[17], (DEPTH, D_S5), 1.0),
        's5_w_glu': nrm(ks[18], (DEPTH, D_S5, D_S5), D_S5 ** -0.5),
        'w_fnet': nrm(ks[19], (DEPTH, N_FNET_GROUPS, FNET_GW, FNET_GW), FNET_GW ** -0.5),
        'w_out': nrm(ks[20], (DEPTH, D, D), D ** -0.5),
        'norm2_g': 1.0 + nrm(ks[21], (DEPTH, D), 0.02),
        'w_router': nrm(ks[22], (DEPTH, D, E), D ** -0.5),
        'b_router': nrm(ks[23], (DEPTH, E), 0.01),
        'w_gate': nrm(ks[24], (DEPTH, E, D, D_FF), D ** -0.5),
        'b_gate': nrm(ks[25], (DEPTH, E, D_FF), 0.01),
        'w_up': nrm(ks[26], (DEPTH, E, D, D_FF), D ** -0.5),
        'b_up': nrm(ks[27], (DEPTH, E, D_FF), 0.01),
        'w_down': nrm(ks[28], (DEPTH, E, D_FF, D), D_FF ** -0.5),
        'b_down': nrm(ks[29], (DEPTH, E, D), 0.01),
        'norm_f_g': 1.0 + nrm(ks[30], (D,), 0.02),
    }

def reference(x_prompt, x_sample, c, state_s5_re, state_s5_im, c_ctx,
              w_ada, b_ada, norm1_g, w_in, s5_lam_re, s5_lam_im, s5_log_dt,
              s5_b_re, s5_b_im, s5_c_re, s5_c_im, s5_d, s5_w_glu, w_fnet, w_out,
              norm2_g, w_router, b_router, w_gate, b_gate, w_up, b_up, w_down, b_down,
              norm_f_g):
    n_prompt = x_prompt.shape[0]
    n_lat = x_sample.shape[1]
    ctx = x_prompt
    lat = x_sample + grid_pos_embed(n_lat, D_MODEL, x_sample.dtype)[None]
    zero_state = jnp.zeros((n_prompt, 2, N_S5_GROUPS, S5_STATE), jnp.float32)
    new_re = []
    new_im = []
    for l in range(DEPTH):
        p = {
            'norm1_g': norm1_g[l], 'w_in': w_in[l],
            'lam_re': s5_lam_re[l], 'lam_im': s5_lam_im[l], 'log_dt': s5_log_dt[l],
            'b_re': s5_b_re[l], 'b_im': s5_b_im[l], 'c_re': s5_c_re[l], 'c_im': s5_c_im[l],
            'd_skip': s5_d[l], 'w_glu': s5_w_glu[l], 'w_fnet': w_fnet[l], 'w_out': w_out[l],
            'norm2_g': norm2_g[l], 'w_router': w_router[l], 'b_router': b_router[l],
            'w_gate': w_gate[l], 'b_gate': b_gate[l], 'w_up': w_up[l], 'b_up': b_up[l],
            'w_down': w_down[l], 'b_down': b_down[l],
        }
        mod_ctx = (jax.nn.silu(c_ctx) @ w_ada[l] + b_ada[l])[None, None, :]
        mod_lat = (jax.nn.silu(c) @ w_ada[l] + b_ada[l])[:, None, :]
        ctx, fin_re, fin_im = trunk_layer(ctx, mod_ctx, zero_state, zero_state, p)
        new_re.append(fin_re)
        new_im.append(fin_im)
        lat, _, _ = trunk_layer(lat, mod_lat, state_s5_re[:, l], state_s5_im[:, l], p)
    y_prompt = rms_norm(ctx, norm_f_g)
    y_sample = rms_norm(lat, norm_f_g)
    new_state_s5_re = jnp.stack(new_re, axis=1)
    new_state_s5_im = jnp.stack(new_im, axis=1)
    return (y_prompt, y_sample, new_state_s5_re, new_state_s5_im)


_drawn_inputs = setup_inputs


def setup_inputs(seed=0):
    import zlib

    import numpy as np

    out = dict(_drawn_inputs(seed))
    spreads = {}
    factors = {'s5_lam_re': 3.835,
     'b_router': 3.139,
     'b_gate': 8.0,
     'b_up': 8.0,
     'b_down': 8.0,
     'norm_f_g': 2.764}
    for name, (base, spread) in spreads.items():
        noise = np.random.default_rng([zlib.crc32(name.encode()), seed]).standard_normal(out[name].shape)
        drawn = base * np.exp(spread * noise) if base else spread * noise
        out[name] = __import__('jax').numpy.asarray(drawn.astype(out[name].dtype))
    for name, factor in factors.items():
        out[name] = (out[name] * factor).astype(out[name].dtype)
    return out
```

```python
import math
from contextlib import ExitStack

import numpy as np

import concourse.bass as bass
from concourse import mybir

F32 = mybir.dt.float32
BF16 = mybir.dt.bfloat16
I32 = mybir.dt.int32
ALU = mybir.AluOpType
ACT = mybir.ActivationFunctionType
AX = mybir.AxisListType

P = 128
D = 1024
L = 128
KD = D // P
CH = 4
NC = L // CH
G = 48
NP = G // 2
HS = 16
ST = 64
DS5 = G * HS
NCT = DS5 // P
TC = 2 * NC
NE = 32
SL_ = 64
NR = NE + 4 * 2 * L // SL_
NRT = NR + 1
HALF = 512
MODW = 256
EPS = 1e-6
TWO_PI = 2.0 * math.pi
C1 = 6.28125
C2 = float(np.float32(np.round((TWO_PI - C1) * 2.0 ** 20) / 2.0 ** 20))
C3 = TWO_PI - C1 - C2
ROUND_MAGIC = 1.5 * 2.0 ** 23

_C = {}
_w = 0
for _n, _k in (("ident", P), ("ones", P), ("ssel", P), ("triu", P), ("cosL", P), ("sinL", P),
               ("ccbd", P), ("nscbd", P), ("wfbd", 2 * P), ("iota", 256), ("eye", NE)):
    _C[_n] = (_w, _w + _k)
    _w += _k
CW = _w


def constant_tile():
    t = np.zeros((P, CW), np.float32)

    def put(name, a):
        t[:a.shape[0], _C[name][0]:_C[name][0] + a.shape[1]] = a

    put("ident", np.eye(P))
    put("ones", np.ones((P, P)))
    ssel = np.zeros((P, P))
    tok_stream = (np.arange(P) // NC) % 2
    for q in range(4):
        for s in range(2):
            ssel[32 * q + s] = tok_stream == s
    put("ssel", ssel)
    put("triu", np.triu(np.ones((P, P)), 1))
    r = np.arange(P)
    tt = CH * (r % NC) + r // NC
    ang = 2 * np.pi * np.outer(tt, tt) / L
    norm = 1.0 / np.sqrt(L * 64.0)
    put("cosL", np.cos(ang) * norm)
    put("sinL", np.sin(ang) * norm)
    ca = 2 * np.pi * np.outer(np.arange(64), np.arange(64)) / 64
    put("ccbd", np.kron(np.eye(2), np.cos(ca)))
    put("nscbd", -np.kron(np.eye(2), np.sin(ca)))
    put("iota", np.tile(np.arange(256.0), (P, 1)))
    put("eye", np.tile(np.eye(NE), (4, 1)))
    return t


def position_table():
    t = np.arange(L)
    q = D // 4
    omega = (np.float32(1.0) / np.float32(10000.0) ** (np.arange(q, dtype=np.float32) / np.float32(q))).astype(np.float32)

    def emb(p):
        a = p.astype(np.float32)[:, None] * omega[None]
        return np.concatenate([np.sin(a), np.cos(a)], -1)

    return np.concatenate([emb(t // 64), emb(t % 64)], -1).astype(np.float32)


def build(nc, cst_d, pos_d, x_prompt, x_sample, c_lat, st_re, st_im, c_ctx, w_ada, b_ada, norm1_g, w_in,
          lam_re, lam_im, log_dt, b_re, b_im, c_re, c_im, d_skip, w_glu, w_fnet, w_out, norm2_g,
          w_router, b_router, w_gate, b_gate, w_up, b_up, w_down, b_down, norm_f_g,
          y_prompt, y_sample, new_re, new_im):
    ctx = ExitStack()
    with ctx:
        BASE = 16512
        SLOT = 4 * D * 4
        RING = BASE
        E_OFF = RING + 3 * SLOT
        W_OFF = RING + 6 * SLOT
        R_OFF = W_OFF + 8 * D * 4
        top = [0]

        def at(name, off, shape, dt=F32):
            n = int(np.prod(shape[1:])) * (2 if dt == BF16 else 4)
            top[0] = max(top[0], off + n)
            return nc.alloc_sbuf_tensor_at(name, shape, dt, offset=off)

        ring = [at(f"ring{i}", RING + i * SLOT, [P, 4, D]) for i in range(6)]
        natB = at("natB", RING, [96, 2 * ST, HS])
        natC = at("natC", RING + 8192, [96, HS, 2, ST])
        ca = at("ca", E_OFF, [P, 2, 2, 5, HS, NP])
        U = at("U", E_OFF + 30720, [P, G, TC])
        DU = at("DU", E_OFF + 30720 + 12288, [P, NP, TC])
        gm = [at(f"gm{d}", E_OFF + 30720 + d * 12288, [P, 2, CH, HS, NP]) for d in range(2)]
        Bt = at("Bt", W_OFF + 6144, [P, HS, 96])
        Ct = at("Ct", W_OFF + 12288, [P, HS, 96])
        h_tok = at("h_tok", W_OFF + 18432, [P, 2, D])
        bbx = [at(f"bbx{d}", (W_OFF + 26624, E_OFF + 30720)[d], [P, NP, 2, 2, HS]) for d in range(2)]
        uc = at("uc", W_OFF, [64, G, 2, CH, HS])
        SL = at("SL", W_OFF, [P, 2, 2, NC + 1, G])
        ufT = at("ufT", W_OFF + 26624, [P, 2, 2, L])
        Zs = at("Zs", W_OFF + 28672, [P, 2, 2, 256])
        wout = at("wout", W_OFF, [P, KD, D])
        GT = at("GT", R_OFF, [P, G, P])
        Zg = at("Zg", R_OFF, [P, NP, TC])
        zc = at("zc", R_OFF + 6144, [64, CH, DS5])
        zT = at("zT", R_OFF + 18432, [P, NCT, 256])
        g1s = at("g1s", R_OFF + 6144, [P, D])
        h2 = at("h2", R_OFF, [P, 2, D])
        bdn = at("bdn", R_OFF + 8192, [NE, D])
        braw = at("braw", R_OFF + 12288, [96, 2, D])
        MISC = R_OFF + 20480
        T_OFF = R_OFF + 24576
        T = at("T", T_OFF, [P, NP, CH * HS])
        bias3 = at("bias3", T_OFF, [96, 2, D], BF16)
        wrt = at("wrt", T_OFF + 4096, [P, KD, NE])
        G_OFF = T_OFF + 6144
        tmpg = at("tmpg", G_OFF, [P, CH, HS, NP])
        KK = at("KK", G_OFF, [P, 6, 7 * HS])
        tmpc = at("tmpc", G_OFF + 6144, [P, 5, HS, NP])
        SM = G_OFF + 6144 + 7680
        wglu = at("wglu", G_OFF, [P, NCT, DS5])
        X_OFF = G_OFF + 18432
        x_tok = at("x_tok", X_OFF, [P, 2, D])
        mod = at("mod", X_OFF + 8192, [P, 6 * MODW])
        HT_OFF = X_OFF + 8192 + 6144
        hT = at("hT", HT_OFF, [P, KD, 256])
        ycT = at("ycT", HT_OFF, [P, KD, 256])
        CO = HT_OFF + 8192
        cst = at("cst", CO, [P, CW])
        CO2 = CO + CW * 4
        gains = at("gains", CO2, [P, 2, MODW])
        cs = at("cs", CO2 + 2048, [P, 46])
        a4r = at("a4r", CO2 + 2048 + 192, [P, G])
        a4i = at("a4i", CO2 + 2048 + 384, [P, 2, G])
        dcol = at("dcol", CO2 + 2048 + 768, [P, NP])
        ss = at("ss", CO2 + 2048 + 864, [P, 8])
        scan_q = at("scan_q", CO2 + 2048 + 896, [P, 2, 2, G])
        scan_p = at("scan_p", W_OFF + 25344, [P, 2, 2, G])
        ist = at("ist", W_OFF + 25344 + 768, [P, 2, G])
        fs = at("fs", R_OFF + 18432, [P, 2, G])
        fso = at("fso", R_OFF + 18432 + 512, [96, P])
        sqj = at("sqj", R_OFF + 12288, [P, D])
        otmp = at("otmp", R_OFF + 10240, [P, HALF])
        g2s = at("g2s", R_OFF + 8192, [P, D])
        assert top[0] <= 229344, top[0]

        def C(name, rows=slice(None)):
            a, b = _C[name]
            return cst[rows, a:b]

        PT = at("PT", SM, [P, 288])
        natL = at("natL", T_OFF, [96, P])
        natS = at("natS", T_OFF + 512, [96, P])
        natT = at("natT", T_OFF + 1024, [G, 2, ST])
        natD = at("natD", T_OFF + 1536, [NP, 2, CH, HS])
        natCc = at("natCc", T_OFF + 2048, [16, P])
        rawT = at("rawT", T_OFF + 2560, [G, 2])
        rawD = at("rawD", T_OFF + 2592, [NP, 2, HS])
        Ap = at("Ap", SM + 1152, [P, 2, 5, G])
        Fp = at("Fp", SM + 1152 + 1920, [P, 2, CH, G])
        sc = at("sc", T_OFF + 2752, [P, 16, G])
        cT = at("cT", T_OFF + 2752 + 3072, [P, 16])

        Xs = at("Xs", G_OFF, [P, HALF])
        XT = at("XT", G_OFF + 2048, [P, 4, P])
        gcl = at("gcl", G_OFF + 4096, [P, HALF])
        sgm = at("sgm", G_OFF + 6144, [P, HALF])
        upc = at("upc", G_OFF + 8192, [P, HALF])
        acts = at("acts", G_OFF + 10240, [P, HALF])
        actT = at("actT", G_OFF + 12288, [P, 4, P])
        ys = at("ys", G_OFF + 14336, [P, HALF])
        sel = at("sel", G_OFF + 16384, [P, 2, SL_])
        selw = at("selw", G_OFF + 16384 + 512, [P, 2, 2, SL_])
        selb = at("selb", G_OFF + 16384 + 1536, [96, SL_], BF16)
        selT = at("selT", T_OFF + 5120, [P, 2 * P])
        lg = at("lg", MISC, [P, 2, NE])
        m8 = at("m8", MISC + 256, [P, 2, 8])
        gt = at("gt", MISC + 320, [P, 2, NE])
        eq = [at(f"eq{i}", MISC + 576 + 256 * i, [P, 2, NE]) for i in range(2)]
        ex = at("ex", MISC + 1088, [P, 2, NE])
        rank = at("rank", MISC + 1344, [P, 2, NE])
        comb = at("comb", MISC + 1600, [P, 2, NE])
        r1c = at("r1c", MISC + 1856, [P, 8])
        cnt = at("cnt", MISC + 1888, [NE, 8])
        cmp = at("cmp", MISC + 1920, [NE, 52])
        brt_f = at("brt_f", MISC + 2944, [1, 64])
        tbl = at("tbl", MISC + 2144, [1, 160], I32)
        brt = at("brt", MISC + 2784, [1, NE])
        combT = at("combT", T_OFF + 5120, [NE, 256])
        r1 = at("r1", G_OFF, [96, 2, D])

        ps = ctx.enter_context(nc.psum_tensor("ps", [P, 8, HALF], F32))
        kd_dram = nc.dram_tensor("k_windows", [G * HS, 7 * HS], F32, kind="Internal").ap()

        S = {}

        def sem(name):
            if name not in S:
                S[name] = ctx.enter_context(nc.semaphore(name))
            return S[name]

        NB = 5
        STAGES = (("params", 1), ("B", 4), ("Cc", 4), ("gt0", 6), ("gt1", 6), ("m12", 1),
                  ("gs1", 4), ("sh1", 4), ("hT", 4), ("u", 4), ("K0", 1), ("K1", 1), ("uf", 1), ("U", 6), ("Z", 2),
                  ("yf", 1), ("loc", 12), ("fin", 1), ("y", 6), ("zc", 6), ("zT", 3), ("glu", 3), ("g1", 4), ("o", 4),
                  ("gs2", 4), ("sh2", 4), ("h2T", 4), ("lg", 1), ("rk", 1), ("cu", 1), ("tb", 1), ("cb", 1))
        first = {}
        njobs = 0
        for n_, k_ in STAGES:
            first[n_] = njobs
            njobs += k_
        bank_full = sem("bank_full")
        bank_drained = [sem(f"bank_drained{b}") for b in range(NB)]

        def bank(stage, i=0):
            return ps[:, (first[stage] + i) % NB, :]

        def claim(pe, stage, i=0):
            n = first[stage] + i
            if n >= NB:
                pe.wait_ge(bank_drained[n % NB], n // NB)
            return ps[:, n % NB, :]

        def filled(eng, stage, i=0):
            eng.wait_ge(bank_full, first[stage] + i + 1)
            return ps[:, (first[stage] + i) % NB, :]

        def drained(ins, stage, i=0):
            ins.then_inc(bank_drained[(first[stage] + i) % NB], 1)

        OUT = [[ps[:, 2 * tau + dh, :] for dh in range(2)] for tau in range(2)]
        pG, pU, pX, pT = (ps[:, b, :] for b in (4, 5, 6, 7))

        early = [("ada", 0, 0), ("ada", 0, 1), ("ada", 1, 0), ("ada", 1, 1), ("w_in", 0, 0), ("w_in", 0, 1)]
        early += [("ada", j, b) for j in range(2, 6) for b in range(2)]
        early_id = {u: n + 1 for n, u in enumerate(early)}
        early_in = [sem(f"early_in{i}") for i in range(3)]
        early_used = [sem(f"early_used{i}") for i in range(3)]

        def early_wait(eng, unit):
            n = early_id[unit]
            eng.wait_ge(early_in[n % 3], 16 * (n // 3 + (1 if n % 3 else 2)))
            return ring[n % 3]

        def early_release(ins, unit):
            ins.then_inc(early_used[early_id[unit] % 3], 1)

        block = ctx.enter_context(nc.Block())

        def tok_rows(j, s):
            b = (j % 2) * 64 + s * 32
            return slice(b, b + 32), j // 2

        W6 = [(w_gate, 0), (w_gate, 1), (w_up, 0), (w_up, 1), (w_down, 0), (w_down, 1)]
        UNITS = ("g0", "g1", "u0", "u1", "d0", "d1")
        unit_in = [sem(f"expert_{u}_in") for u in UNITS]
        unit_used = [sem(f"expert_{u}_used") for u in UNITS]

        def halves(w, e, b):
            return w[0, e].rearrange("(b k p) c -> b p k c", b=2, p=P)[b]

        @block.sync
        def _(sp):
            def load(dst, src, s):
                sp.dma_start(dst, src).then_inc(sem(s), 16)

            load(cst[:, :], cst_d, "cst_in")
            for half, t in ((0, lam_re), (1, lam_im)):
                load(natL[half * G:(half + 1) * G, :], t.rearrange("a d (k g) p -> (a d k) (g p)", g=2), "small_in")
            for half, t in ((0, st_re), (1, st_im)):
                load(natS[half * G:(half + 1) * G, :], t.rearrange("a b d (k g) p -> (a b d k) (g p)", g=2), "small_in")
            load(rawT[:, :], log_dt.rearrange("a d (k g) -> (a d k) g", g=2), "small_in")
            load(rawD[:, :, :], d_skip.rearrange("a (k g h) -> (a k) g h", g=2, h=HS), "small_in")
            load(natCc[0:8, :], c_ctx.rearrange("(k p) -> k p", p=P), "small_in")
            load(natCc[8:16, :], c_lat.rearrange("a (k p) -> (a k) p", p=P), "small_in")
            for half, t in ((0, b_re), (1, b_im)):
                sp.dma_start(natB[half * G:(half + 1) * G, :, :],
                             t.rearrange("a d (k g) p h -> (a d k) (g p) h", g=2)).then_inc(early_in[0], 16)
            for half, t in ((0, c_re), (1, c_im)):
                for g2 in range(2):
                    sp.dma_start(natC[half * G:(half + 1) * G, :, g2, :],
                                 t.rearrange("a d (k g) h p -> g (a d k) h p", g=2)[g2]).then_inc(sem("natC_in"), 16)
            for j in range(CH):
                for s, t in ((0, x_prompt), (1, x_sample)):
                    rows, tau = tok_rows(j, s)
                    load(x_tok[rows, tau, :], t[0].rearrange("(c j) d -> j c d", j=CH)[j], "x_in")
            for j in range(CH):
                rows, tau = tok_rows(j, 1)
                load(h_tok[rows, tau, :], pos_d.rearrange("(c j) d -> j c d", j=CH)[j], "pos_in")
            sp.wait_ge(sem("cleared"), 4)
            sp.wait_ge(sem("cst_in"), 16)
            for s in range(2):
                for ch in range(6):
                    load(mod[s:P:32, ch * MODW:(ch + 1) * MODW],
                         b_ada[0, ch * D:(ch + 1) * D].rearrange("(q i) -> q i", q=4), "rows_in")
                for n, t in ((0, norm1_g), (1, norm2_g)):
                    load(gains[s:P:32, n, :], t[0].rearrange("(q i) -> q i", q=4), "rows_in")
            for g in range(4):
                lo = _C["wfbd"][0] + (g // 2) * P + (g % 2) * 64
                load(cst[64 * (g % 2):64 * (g % 2) + 64, lo:lo + 64], w_fnet[0, g], "wf_in")
            for n, (kind, j, b) in enumerate(early):
                u = n + 1
                if u >= 3:
                    sp.wait_ge(early_used[u % 3], u // 3)
                w = w_ada[0, :, j * D:(j + 1) * D] if kind == "ada" else w_in[0]
                sp.dma_start(ring[u % 3][:, :, :], w.rearrange("(b k p) c -> b p k c", b=2, p=P)[b])\
                  .then_inc(early_in[u % 3], 16)
            sp.wait_ge(sem("kd_out"), 16)
            sp.wait_ge(sem("scratch_dead"), 1)
            load(wglu[:, :, :], w_glu[0].rearrange("(k p) c -> p k c", p=P), "wglu_in")
            for i in range(3):
                last = max(n for n in early_id.values() if n % 3 == i)
                sp.wait_ge(early_used[i], last // 3 + 1)
                sp.dma_start(ring[i][:, :, :], halves(W6[i][0], 0, W6[i][1])).then_inc(unit_in[i], 16)
            sp.wait_ge(sem("s5_read"), 1)
            sp.wait_ge(sem("du_dead"), 6)
            load(wout[:, :, :], w_out[0].rearrange("(k p) c -> p k c", p=P), "wout_in")
            for i in range(3, 6):
                sp.dma_start(ring[i][:, :, :], halves(W6[i][0], 0, W6[i][1])).then_inc(unit_in[i], 16)
            load(wrt[:, :, :], w_router[0].rearrange("(k p) e -> p k e", p=P), "route_in")
            sp.wait_ge(sem("x2_ready"), 4)
            sp.wait_ge(sem("ss_ready"), 4)
            load(brt[:, :], b_router, "route_in")
            load(bdn[:, :], b_down[0], "route_in")
            for n in range(3):
                for i, t in ((0, b_gate), (1, b_up)):
                    load(braw[NE * n:NE * (n + 1), i, :], t[0], "braw_in")
            sp.wait_ge(sem("gain_dead"), 1)
            for s in range(2):
                load(gains[s:P:32, 0, :], norm_f_g.rearrange("(q i) -> q i", q=4), "gainf_in")
            sp.wait_ge(sem("tables"), 1)
            with sp.Fori(1, NE) as e:
                done = sp.value_load(tbl[0:1, bass.ds(e + (2 * NRT + 1), 1)], min_val=1, max_val=NR)
                for i in range(6):
                    sp.wait_ge(unit_used[i], done)
                    w = W6[i][0][0].rearrange("e (b k p) c -> e b p k c", b=2, p=P)
                    sp.dma_start(ring[i][:, :, :],
                                 w[bass.ds(e, 1), W6[i][1]].rearrange("e p k c -> (e p) k c")).then_inc(unit_in[i], 16)
            sp.wait_ge(sem("y_ready"), 2)
            for j in range(CH):
                for s, t in ((0, y_prompt), (1, y_sample)):
                    rows, tau = tok_rows(j, s)
                    sp.dma_start(t[0].rearrange("(c j) d -> j c d", j=CH)[j], h2[rows, tau, :])\
                      .then_inc(sem("y_out"), 16)
            sp.wait_ge(sem("y_out"), 16 * 8)

        def scan(eng, link, d):
            tp, tq = scan_p[:, d], scan_q[:, d]
            ar = a4r[:, d * NP:(d + 1) * NP].unsqueeze(2).broadcast_to([P, NP, 2])
            ar2 = ar.unsqueeze(1).broadcast_to([P, 2, NP, 2])
            ai2 = a4i[:, :, d * NP:(d + 1) * NP].unsqueeze(3).broadcast_to([P, 2, NP, 2])
            v = lambda a: a.rearrange("p r (k s) -> p r k s", s=2)
            for step in range(NC):
                prev, cur = (step, step + 1) if d == 0 else (NC - step, NC - 1 - step)
                xp, xc = SL[:, :, d, prev, :], SL[:, :, d, cur, :]
                xs = SL[:, ::-1, d, prev, :]
                link(eng.tensor_tensor(v(tp), ar2, v(xp), ALU.mult))
                link(eng.tensor_tensor(v(tq), ai2, v(xs), ALU.mult))
                link(eng.tensor_tensor(tp, tp, tq, ALU.add))
                link(eng.tensor_tensor(xc, xc, tp, ALU.add))

        def loc_out(copy, b, kb, r):
            for d in range(2):
                o = SL[:, r, d, 1 - d:1 - d + NC, 8 * kb:8 * kb + 8].rearrange("p c x -> p x c")
                ins = copy(o, b[:, d * 256:(d + 1) * 256].rearrange("p (x c) -> p x c", c=NC))
            return ins

        def twice(b):
            return b.rearrange("p (g h) -> p g h", h=HS).unsqueeze(2).broadcast_to([64, 24, 2, HS])

        def zc_view(i):
            return zc[:, :, P * i:P * (i + 1)].rearrange("p j (g h) -> p g j h", h=HS)

        @block.gpsimd
        def _(pool):
            n = [0]

            def link(ins):
                n[0] += 1
                ins.then_inc(sem("pool_chain"), 1)
                pool.wait_ge(sem("pool_chain"), n[0])

            pool.memset(mod[:, :], 0.0).then_inc(sem("cleared"), 1)
            pool.memset(gains[:, :, :], 0.0).then_inc(sem("cleared"), 1)
            pool.memset(bbx[0][:, :, :, :, :], 0.0).then_inc(sem("cleared"), 1)
            pool.memset(cs[:, :], 0.0).then_inc(sem("cleared"), 1)
            pool.wait_ge(sem("small_in"), 16 * 8)
            pool.tensor_copy(natT[:, :, :], rawT[:, :].unsqueeze(2).broadcast_to([G, 2, ST])).then_inc(sem("nat_rep"), 1)
            pool.tensor_copy(natD[:, :, :, :], rawD[:, :, :].unsqueeze(2).broadcast_to([NP, 2, CH, HS]))\
                .then_inc(sem("nat_rep"), 1)
            pool.wait_ge(sem("nat_rep"), 2)
            pool.wait_ge(sem("x_in"), 16 * 8)
            pool.wait_ge(sem("pos_in"), 16 * 4)
            for j in range(CH):
                rows, tau = tok_rows(j, 1)
                pool.tensor_tensor(x_tok[rows, tau, :], x_tok[rows, tau, :], h_tok[rows, tau, :], ALU.add)\
                    .then_inc(sem("pos_added"), 1)
                pool.wait_ge(sem("pos_added"), j + 1)
            pool.wait_ge(sem("powers"), 2)
            pool.wait_ge(sem("Ct_ready"), 4)
            for d in range(2):
                step = slice(None) if d == 0 else slice(None, None, -1)
                ar, ai = (Ap[:, r, step, d * NP:(d + 1) * NP].unsqueeze(2).broadcast_to([P, 5, HS, NP]) for r in range(2))
                cr, ci = (Ct[:, :, r * G + d * NP:r * G + (d + 1) * NP].unsqueeze(1).broadcast_to([P, 5, HS, NP])
                          for r in range(2))
                re, im = ca[:, d, 0], ca[:, d, 1]
                link(pool.tensor_tensor(re, cr, ar, ALU.mult))
                link(pool.tensor_tensor(tmpc[:, :, :, :], ci, ai, ALU.mult))
                link(pool.tensor_tensor(re, re, tmpc[:, :, :, :], ALU.subtract))
                link(pool.tensor_tensor(im, cr, ai, ALU.mult))
                link(pool.tensor_tensor(tmpc[:, :, :, :], ci, ar, ALU.mult))
                link(pool.tensor_tensor(tmpc[:, :, :, :], im, tmpc[:, :, :, :], ALU.add))
                link(pool.tensor_scalar(im, tmpc[:, :, :, :], -1.0, None, ALU.mult))
                pool.sem_inc(sem("ca_ready"), 1)
            pool.wait_ge(sem("windows"), 2)
            pool.dma_start(kd_dram.rearrange("(b r) c -> r b c", r=P), KK[:, :, :]).then_inc(sem("kd_out"), 16)
            pool.wait_ge(sem("kd_out"), 16)
            win = kd_dram.rearrange("(k g h) c -> g h k c", g=2, h=HS)
            for g2 in range(2):
                for j in range(CH):
                    r0 = 64 * g2 + 16 * j
                    pool.dma_start(T[r0:r0 + 16, :, :], win[g2, :, :, (3 - j) * HS:(7 - j) * HS])\
                        .then_inc(sem("T_in"), 16)
            pool.wait_ge(sem("U_ready"), 6)
            for g2 in range(2):
                rows = slice(64 * g2, 64 * g2 + 64)
                pool.tensor_tensor(DU[rows, :, :], U[rows, g2::2, :],
                                   dcol[rows, :].unsqueeze(2).broadcast_to([64, NP, TC]), ALU.mult)\
                    .then_inc(sem("du_ready"), 1)
                pool.wait_ge(sem("du_ready"), g2 + 1)
            pool.wait_ge(sem("loc_ready_act"), 6)
            pool.wait_ge(sem("loc_ready_dve"), 6)
            pool.wait_ge(sem("init_ready"), 1)
            scan(pool, link, 1)
            pool.sem_inc(sem("scan_pool"), 1)
            pool.wait_ge(sem("braw_in"), 16 * 6)
            pool.wait_ge(sem("y_filled"), 1)
            pool.wait_ge(sem("glu_filled"), 1)
            link(pool.tensor_copy(bias3[:, :, :], braw[:, :, :]))
            link(pool.tensor_tensor(r1[:, :, :], braw[:, :, :], bias3[:, :, :], ALU.subtract))
            for lo in (32, 64):
                link(pool.tensor_copy(bias3[lo:lo + 32, :, :], r1[lo:lo + 32, :, :]))
            link(pool.tensor_tensor(r1[64:96, :, :], r1[64:96, :, :], bias3[64:96, :, :], ALU.subtract))
            pool.tensor_copy(bias3[64:96, :, :], r1[64:96, :, :]).then_inc(sem("bias_ready"), 1)


        @block.tensor
        def _(pe):
            ident = C("ident")

            def tr(out, src, last=None):
                k = src.shape[0]
                return pe.transpose(out, src, ident[0:k, 0:k])

            def full(ins):
                ins.then_inc(bank_full, 1)

            pe.wait_ge(sem("cst_in"), 16)
            pe.wait_ge(sem("small_in"), 16 * 8)
            pe.wait_ge(sem("nat_rep"), 2)
            b = claim(pe, "params")
            tr(b[:, 0:96], natL[:, :])
            tr(b[:, 96:192], natS[:, :])
            tr(b[:, 192:240], natT[:, :, :].rearrange("r g p -> r (g p)"))
            tr(b[:, 240:264], natD[:, :, :, :].rearrange("r g i h -> r (g i h)"))
            full(tr(b[:, 264:280], natCc[:, :]))
            pe.wait_ge(early_in[0], 32)
            for i in range(4):
                b = claim(pe, "B", i)
                for n in range(4):
                    ins = tr(b[:, n * 96:(n + 1) * 96], natB[:, :, 4 * i + n])
                full(ins)
            pe.wait_ge(sem("natC_in"), 64)
            for i in range(4):
                b = claim(pe, "Cc", i)
                for n in range(4):
                    ins = tr(b[:, n * 96:(n + 1) * 96], natC[:, 4 * i + n, :, :].rearrange("r g p -> r (g p)"))
                full(ins)
            pe.wait_ge(bank_full, first["Cc"] + 4)
            pe.sem_inc(early_used[0], 1)

            def mod_chunk(j):
                pe.wait_ge(sem("cs_ready"), 1)
                out = ps[:, 5 + j // 2, (j % 2) * MODW:(j % 2 + 1) * MODW]
                for b_ in range(2):
                    w = early_wait(pe, ("ada", j, b_))
                    for k in range(4):
                        kk = 4 * b_ + k
                        for q in range(4):
                            ins = pe.matmul(out[32 * q:32 * q + 32, :], cs[:, 2 * kk:2 * kk + 32],
                                            w[:, k, q * MODW:(q + 1) * MODW], start=(kk == 0), stop=(kk == 7),
                                            skip_group_check=True)
                    early_release(ins, ("ada", j, b_))
                pe.wait_ge(early_used[early_id[("ada", j, 1)] % 3], early_id[("ada", j, 1)] // 3 + 1)
                pe.sem_inc(sem("mod_filled"), 1)

            def gt_tables(d):
                pe.wait_ge(sem("gm_ready"), d + 1)
                g = gm[d][:, :, :, :, :].rearrange("p r j h k -> p (r j h) k")
                for i in range(6):
                    b = claim(pe, f"gt{d}", i)
                    for n in range(4):
                        ins = tr(b[:, n * P:(n + 1) * P], g[:, :, 4 * i + n])
                    full(ins)

            def spread(stage, rows):
                for q in range(4):
                    b = claim(pe, stage, q)
                    full(pe.matmul(b[:, 0:MODW], C("ssel", slice(32 * q, 32 * q + 32)), rows[32 * q:32 * q + 32, :],
                                   start=True, stop=True))

            mod_chunk(0)
            gt_tables(0)
            mod_chunk(1)
            gt_tables(1)
            pe.wait_ge(sem("wf_in"), 16 * 4)
            b = claim(pe, "m12")
            for t in range(2):
                wf = C("wfbd")[:, t * P:(t + 1) * P]
                pe.matmul(b[:, t * 256:t * 256 + P], C("ccbd"), wf, start=True, stop=True)
                ins = pe.matmul(b[:, t * 256 + P:(t + 1) * 256], C("nscbd"), wf, start=True, stop=True)
            full(ins)
            pe.wait_ge(sem("mod_rows"), 2)
            spread("gs1", mod[:, MODW:2 * MODW])
            spread("sh1", mod[:, 0:MODW])

            def turn_tokens(stage, src, ready):
                pe.wait_ge(sem(ready), 8)
                for i in range(4):
                    b = claim(pe, stage, i)
                    for k in range(2):
                        for tau in range(2):
                            ins = tr(b[:, k * 256 + tau * P:k * 256 + (tau + 1) * P],
                                     src[:, tau, (2 * i + k) * P:(2 * i + k + 1) * P])
                    full(ins)

            turn_tokens("hT", h_tok, "h_ready")
            w0 = early_wait(pe, ("w_in", 0, 0))
            w1 = early_wait(pe, ("w_in", 0, 1))
            pe.wait_ge(sem("hT_ready"), 4)
            for tau in range(2):
                for n in range(2):
                    b = claim(pe, "u", 2 * tau + n)
                    for k in range(KD):
                        w = (w0, w1)[k // 4]
                        ins = pe.matmul(b[:, 0:384], hT[:, k, tau * P:(tau + 1) * P], w[:, k % 4, n * 384:(n + 1) * 384],
                                        start=(k == 0), stop=(k == KD - 1))
                    full(ins)
            for d in range(2):
                pe.wait_ge(sem("bbx_ready"), d + 1)
                pe.wait_ge(sem("ca_ready"), d + 1)
                b = claim(pe, f"K{d}")
                m0 = 0 if d == 0 else 1
                for k in range(NP):
                    q, kb = k % 4, k // 4
                    for r in range(2):
                        ins = pe.matmul(b[32 * q:32 * q + 32, kb * 64:kb * 64 + 64],
                                        bbx[d][:, k, r, :, :].rearrange("p g h -> p (g h)"),
                                        ca[:, d, r, m0:m0 + 4, :, k].rearrange("p m h -> p (m h)"),
                                        start=(r == 0), stop=(r == 1))
                full(ins)
            b = claim(pe, "uf")
            for t in range(2):
                for k in range(KD):
                    w = (w0, w1)[k // 4]
                    ins = pe.matmul(b[:, t * 256:(t + 1) * 256], w[:, k % 4, DS5 + t * P:DS5 + (t + 1) * P], hT[:, k, :],
                                    start=(k == 0), stop=(k == KD - 1))
            full(ins)
            pe.wait_ge(bank_full, first["uf"] + 1)
            pe.sem_inc(early_used[early_id[("w_in", 0, 0)] % 3], 1)
            pe.sem_inc(early_used[early_id[("w_in", 0, 1)] % 3], 1)
            pe.wait_ge(sem("uc_ready_dve"), 4)
            pe.wait_ge(sem("uc_ready_act"), 4)
            for i in range(6):
                b = claim(pe, "U", i)
                for n in range(8):
                    ins = tr(b[:, n * 64:(n + 1) * 64], uc[:, 8 * i + n, :, :, :].rearrange("p r j h -> p (r j h)"))
                full(ins)
            pe.wait_ge(sem("ufT_ready"), 1)
            pe.wait_ge(sem("m12_ready"), 1)
            m12 = cst[:, _C["ccbd"][0]:_C["ccbd"][0] + 512]
            for s in range(2):
                b = claim(pe, "Z", s)
                for t in range(2):
                    ins = pe.matmul(b[:, t * 256:(t + 1) * 256], ufT[:, t, s, :], m12[:, t * 256:(t + 1) * 256], start=True, stop=True)
                full(ins)
            pe.wait_ge(sem("Zs_ready"), 2)
            b = claim(pe, "yf")
            for t in range(2):
                for s in range(2):
                    o = b[:, t * 256:(t + 1) * 256].rearrange("p (j s c) -> p s j c", s=2, c=NC)[:, s]
                    pe.matmul(o, Zs[:, s, t, 0:P], C("cosL"), start=True, stop=False)
                    ins = pe.matmul(o, Zs[:, s, t, P:2 * P], C("sinL"), start=False, stop=True)
            full(ins)
            pe.wait_ge(sem("U_ready"), 6)
            pe.wait_ge(sem("GT_ready"), 12)
            for kb in range(6):
                for r in range(2):
                    b = claim(pe, "loc", 2 * kb + r)
                for d in range(2):
                    for q in range(4):
                        k = 4 * kb + q
                        for g2 in range(2):
                            for r in range(2):
                                rows = slice(64 * r, 64 * r + 64)
                                last_r = pe.matmul(
                                    bank("loc", 2 * kb + r)[64 * g2:64 * g2 + 64, (4 * d + q) * 64:(4 * d + q + 1) * 64],
                                    GT[rows, d * NP + k, 64 * g2:64 * g2 + 64], U[rows, 2 * k + g2, :],
                                    start=True, stop=True)
                                if d == 1 and q == 3 and g2 == 1:
                                    full(last_r)
            for j in range(2, 6):
                mod_chunk(j)
            pe.wait_ge(sem("fs_ready"), 1)
            b = claim(pe, "fin")
            full(tr(b[0:96, 0:P], fs[:, :, :].rearrange("p r k -> p (r k)")))
            pe.wait_ge(sem("T_in"), 16 * 8)
            pe.wait_ge(sem("scan_dve"), 1)
            pe.wait_ge(sem("scan_pool"), 1)
            for kb in range(3):
                for g2 in range(2):
                    claim(pe, "y", 2 * kb + g2)
                for kk in range(8):
                    k = 8 * kb + kk
                    for n in range(5):
                        for g2 in range(2):
                            rows = slice(64 * g2, 64 * g2 + 64)
                            o = bank("y", 2 * kb + g2)[rows, kk * 64:(kk + 1) * 64]
                            if n == 0:
                                ins = pe.matmul(o, T[rows, k, :], U[rows, 2 * k + g2, :], start=True, stop=False)
                                continue
                            d, r = (n - 1) // 2, (n - 1) % 2
                            m0 = 1 if d == 0 else 0
                            lhs = ca[rows, d, r, m0:m0 + 4, :, k].rearrange("p m h -> p (m h)")
                            st = SL[rows, r, d, d:d + NC, 2 * k:2 * k + 2].rearrange("p c s -> p s c")
                            ins = pe.matmul(o, lhs, st, start=False, stop=(n == 4))
                            if n == 4 and kk == 7:
                                full(ins)
            pe.wait_ge(bank_full, first["y"] + 6)
            pe.sem_inc(sem("s5_read"), 1)
            pe.sem_inc(sem("y_filled"), 1)
            for i in range(6):
                pe.wait_ge(sem("z_ready"), 2 * (i // 2) + 2)
                b = claim(pe, "zc", i)
                for n in range(4):
                    ins = tr(b[0:64, n * P:(n + 1) * P], Zg[:, 4 * i + n, :])
                full(ins)
            pe.wait_ge(sem("zc_ready"), 6)
            for i in range(3):
                b = claim(pe, "zT", i)
                for t in range(2):
                    for j in range(CH):
                        ct = 2 * i + t
                        ins = tr(b[:, t * 256 + j * 64:t * 256 + (j + 1) * 64], zc[:, j, ct * P:(ct + 1) * P])
                full(ins)
            pe.wait_ge(sem("wglu_in"), 16)
            pe.wait_ge(sem("zT_ready"), 3)
            for i in range(3):
                b = claim(pe, "glu", i)
                for t in range(2):
                    ct = 2 * i + t
                    for k in range(NCT):
                        ins = pe.matmul(b[:, t * 256:(t + 1) * 256], wglu[:, k, ct * P:(ct + 1) * P], zT[:, k, :],
                                        start=(k == 0), stop=(k == NCT - 1))
                full(ins)
            pe.wait_ge(bank_full, first["glu"] + 3)
            pe.sem_inc(sem("glu_filled"), 1)
            pe.wait_ge(sem("mod_rows"), 6)
            spread("g1", mod[:, 2 * MODW:3 * MODW])
            pe.wait_ge(sem("wout_in"), 16)
            pe.wait_ge(sem("yc_ready"), 3)
            pe.wait_ge(sem("yf_ready"), 1)
            for tau in range(2):
                for dh in range(2):
                    b = claim(pe, "o", 2 * tau + dh)
                    for k in range(KD):
                        ins = pe.matmul(b, ycT[:, k, tau * P:(tau + 1) * P], wout[:, k, dh * HALF:(dh + 1) * HALF],
                                        start=(k == 0), stop=(k == KD - 1))
                    full(ins)
            spread("gs2", mod[:, 4 * MODW:5 * MODW])
            spread("sh2", mod[:, 3 * MODW:4 * MODW])
            turn_tokens("h2T", h2, "h2_ready")
            pe.wait_ge(sem("route_in"), 16 * 3)
            pe.wait_ge(sem("h2T_ready"), 4)
            b = claim(pe, "lg")
            for tau in range(2):
                o = b[:, tau * NE:(tau + 1) * NE]
                pe.matmul(o, C("ones", slice(0, 1)), brt[:, :], start=True, stop=False)
                for k in range(KD):
                    ins = pe.matmul(o, hT[:, k, tau * P:(tau + 1) * P], wrt[:, k, :], start=False, stop=(k == KD - 1))
            full(ins)
            pe.wait_ge(sem("mask_ready"), 1)
            b = claim(pe, "rk")
            pe.matmul(b[:, 0:NE], C("triu"), gt[:, 0, :], start=True, stop=True)
            pe.matmul(b[:, NE:2 * NE], C("ones"), gt[:, 0, :], start=True, stop=False)
            pe.matmul(b[:, NE:2 * NE], C("triu"), gt[:, 1, :], start=False, stop=True)
            for tau in range(2):
                ins = pe.matmul(b[0:NE, 64:65], gt[:, tau, :], C("ones")[:, 0:1], start=(tau == 0), stop=(tau == 1))
            full(ins)
            pe.wait_ge(sem("rounds_ready"), 1)
            b = claim(pe, "cu")
            full(pe.matmul(b[0:NE, 0:1], C("triu", slice(0, NE))[:, 0:NE], cnt[:, 1:2], start=True, stop=True))
            pe.wait_ge(sem("cmp_ready"), 1)
            b = claim(pe, "tb")
            pe.matmul(b[0:1, 0:NRT], C("ones", slice(0, NE))[:, 0:1], cmp[:, 0:NRT], start=True, stop=True)
            pe.matmul(b[0:1, NRT:2 * NRT], cnt[:, 1:2], cmp[:, 0:NRT], start=True, stop=True)
            pe.matmul(b[0:1, 2 * NRT:2 * NRT + 1], cnt[:, 1:2], C("ones", slice(0, NE))[:, 0:1], start=True, stop=True)
            full(pe.matmul(b[0:1, 2 * NRT + 1:2 * NRT + 1 + NE], cnt[:, 1:2], C("triu", slice(0, NE))[:, 0:NE],
                           start=True, stop=True))
            pe.wait_ge(sem("comb_ready"), 1)
            b = claim(pe, "cb")
            for tau in range(2):
                ins = tr(b[0:NE, tau * P:(tau + 1) * P], comb[:, tau, :])
            full(ins)
            pe.wait_ge(sem("combT_ready"), 1)
            for bb in range(NB):
                pe.wait_ge(bank_drained[bb], len([n for n in range(njobs) if n % NB == bb]))
            for tau in range(2):
                for dh in range(2):
                    pe.matmul(OUT[tau][dh], combT[:, tau * P:(tau + 1) * P], bdn[:, dh * HALF:(dh + 1) * HALF],
                              start=True, stop=False, skip_group_check=True)
            pe.wait_ge(sem("tables"), 1)
            total = pe.value_load(tbl[0:1, 2 * NRT:2 * NRT + 1], min_val=NE, max_val=NR)

            def gather(r):
                pe.wait_ge(sem("sel_ready"), r + 1)
                for tau in range(2):
                    for dh in range(2):
                        ins = pe.matmul(pX[64 * dh:64 * dh + 64, :], sel[:, tau, :],
                                        h2[:, tau, dh * HALF:(dh + 1) * HALF], start=(tau == 0), stop=(tau == 1),
                                        skip_group_check=True)
                ins.then_inc(sem("gathered"), 1)
                pe.wait_ge(sem("Xs_ready"), r + 1)
                for n in range(4):
                    ins = tr(pT[:, n * P:(n + 1) * P], Xs[:, n * P:(n + 1) * P])
                ins.then_inc(sem("X_turned"), 1)

            def turn_sel(r):
                pe.wait_ge(sem("sel_ready"), r + 1)
                for tau in range(2):
                    ins = tr(pX[:, tau * P:(tau + 1) * P], selw[:, tau, :, :].rearrange("p a b -> p (a b)"))
                ins.then_inc(sem("sel_turned"), 1)

            gather(0)
            turn_sel(0)
            pe.wait_ge(sem("bias_ready"), 1)
            with pe.Fori(0, total) as R:
                e = pe.value_load(tbl[0:1, bass.ds(R, 1)], min_val=0, max_val=NE - 1)
                pe.wait_ge(sem("XT_ready"), R + 1)
                pe.wait_ge(sem("selb_ready"), R + 1)
                for m, out in ((0, pG), (1, pU)):
                    for fh in range(2):
                        pe.matmul(out[64 * fh:64 * fh + 64, :], selb[:, :], bias3[:, m, fh * HALF:(fh + 1) * HALF],
                                  start=True, stop=False, skip_group_check=True)
                    for k in range(KD):
                        i = 2 * m + k // 4
                        if k % 4 == 0:
                            pe.wait_ge(unit_in[i], 16 * e + 16)
                        for fh in range(2):
                            ins = pe.matmul(out[64 * fh:64 * fh + 64, :], XT[:, k % 4, (k // 4) * 64:(k // 4) * 64 + 64],
                                            ring[i][:, k % 4, fh * HALF:(fh + 1) * HALF], start=False,
                                            stop=(k == KD - 1), skip_group_check=True)
                        if k % 4 == 3:
                            ins.then_inc(unit_used[i], 1)
                pe.wait_ge(sem("selT_ready"), R + 1)
                gather(R + 1)
                pe.wait_ge(sem("XT_ready"), R + 2)
                pe.wait_ge(sem("act_ready"), R + 1)
                for n in range(4):
                    ins = tr(pT[:, n * P:(n + 1) * P], acts[:, n * P:(n + 1) * P])
                ins.then_inc(sem("act_turned"), 1)
                pe.wait_ge(sem("actT_ready"), R + 1)
                for k in range(KD):
                    i = 4 + k // 4
                    if k % 4 == 0:
                        pe.wait_ge(unit_in[i], 16 * e + 16)
                    for dh in range(2):
                        ins = pe.matmul(pX[64 * dh:64 * dh + 64, :], actT[:, k % 4, (k // 4) * 64:(k // 4) * 64 + 64],
                                        ring[i][:, k % 4, dh * HALF:(dh + 1) * HALF], start=(k == 0), stop=(k == KD - 1),
                                        skip_group_check=True)
                    if k % 4 == 3:
                        ins.then_inc(unit_used[i], 1)
                pe.wait_ge(sem("ys_ready"), R + 1)
                for tau in range(2):
                    for dh in range(2):
                        rows = slice(64 * dh, 64 * dh + 64)
                        ins = pe.matmul(OUT[tau][dh], selT[rows, tau * P:(tau + 1) * P], ys[rows, :],
                                        start=False, stop=False, skip_group_check=True)
                ins.then_inc(sem("scattered"), 1)
                turn_sel(R + 1)
            pe.wait_ge(sem("gainf_in"), 32)
            pe.wait_ge(sem("selT_ready"), total + 1)
            pe.wait_ge(sem("XT_ready"), total + 1)
            for q in range(4):
                rows = slice(32 * q, 32 * q + 32)
                pe.matmul(ps[:, 4 + q, 0:MODW], C("ssel", rows), mod[rows, 5 * MODW:6 * MODW], start=True, stop=True)
                ins = pe.matmul(ps[:, 4 + q, MODW:2 * MODW], C("ssel", rows), gains[rows, 0, :], start=True, stop=True)
            ins.then_inc(sem("end_rows"), 1)

        @block.scalar
        def _(act):
            act.wait_ge(sem("PT_ready"), 1)
            act.activation(sc[:, 1, :], PT[:, 192:240], ACT.Exp).then_inc(sem("dt_ready"), 1)
            act.wait_ge(sem("er_ready"), 1)
            act.activation(sc[:, 4, :], sc[:, 3, :], ACT.Exp).then_inc(sem("mag_ready"), 1)
            act.activation(cT[:, :], PT[:, 264:280], ACT.Sigmoid).then_inc(sem("sig_ready"), 1)
            act.wait_ge(sem("angle_ready"), 1)
            act.activation(sc[:, 8:10, :], sc[:, 6:8, :], ACT.Sin).then_inc(sem("sin_ready"), 1)
            for i in range(4):
                b = filled(act, "Cc", i)
                ins = act.copy(Ct[:, 4 * i:4 * i + 4, :], b[:, 0:384].rearrange("p (h x) -> p h x", x=96))
                drained(ins, "Cc", i)
            act.wait_ge(bank_drained[(first["Cc"] + 3) % NB], (first["Cc"] + 3) // NB + 1)
            act.sem_inc(sem("Ct_ready"), 4)
            act.wait_ge(sem("pos_added"), 4)
            for tau in range(2):
                act.activation(h_tok[:, tau, :], x_tok[:, tau, :], ACT.Square, accum_out=ss[:, tau:tau + 1])\
                    .then_inc(sem("ss_ready"), 1)
            for d in range(2):
                if d == 1:
                    act.wait_ge(sem("ms_ready"), 1)
                    act.activation(ss[:, 4:6], ss[:, 2:4], ACT.Sqrt).then_inc(sem("rms_ready"), 1)
                for i in range(6):
                    b = filled(act, f"gt{d}", i)
                    k = d * NP + 4 * i
                    drained(act.copy(GT[:, k:k + 4, :], b.rearrange("p (k x) -> p k x", x=P)), f"gt{d}", i)
            act.wait_ge(bank_drained[(first["gt1"] + 5) % NB], (first["gt1"] + 5) // NB + 1)
            act.sem_inc(sem("GT_ready"), 12)
            for i in (1, 3):
                b = filled(act, "hT", i)
                ins = act.copy(hT[:, 2 * i:2 * i + 2, :], b.rearrange("p (k x) -> p k x", x=256))
                drained(ins, "hT", i)
                act.wait_ge(bank_drained[(first["hT"] + i) % NB], (first["hT"] + i) // NB + 1)
                act.sem_inc(sem("hT_ready"), 1)

            def copy_signal(dst, src, stage, i, s):
                drained(act.copy(dst, src), stage, i)
                n = first[stage] + i
                act.wait_ge(bank_drained[n % NB], n // NB + 1)
                act.sem_inc(sem(s), 1)

            act.wait_ge(sem("uc_free"), 1)
            for i in range(4):
                b = filled(act, "u", i)
                tau, n = i // 2, i % 2
                act.copy(uc[:, 24 * n:24 * n + 24, :, 2 * tau + 1, :], twice(b[64:128, 0:384]))\
                    .then_inc(sem("uc_ready_act"), 1)
            b = filled(act, "uf")
            for t in range(2):
                ins = act.copy(ufT[:, t, :, :].rearrange("p s (j c) -> p s j c", c=NC),
                               b[:, t * 256:(t + 1) * 256].rearrange("p (j s c) -> p s j c", s=2, c=NC))
            drained(ins, "uf")
            act.wait_ge(bank_drained[first["uf"] % NB], first["uf"] // NB + 1)
            act.sem_inc(sem("ufT_ready"), 1)
            for i in (1, 3, 5):
                b = filled(act, "U", i)
                copy_signal(U[:, 8 * i:8 * i + 8, :], b.rearrange("p (g x) -> p g x", x=TC), "U", i, "U_ready")
            for s in range(2):
                b = filled(act, "Z", s)
                copy_signal(Zs[:, s, :, :], b.rearrange("p (t x) -> p t x", x=256), "Z", s, "Zs_ready")
            b = filled(act, "yf")
            copy_signal(ycT[:, NCT:KD, :], b.rearrange("p (t x) -> p t x", x=256), "yf", 0, "yf_ready")
            act.wait_ge(sem("U_ready"), 6)
            for kb in range(6):
                b = filled(act, "loc", 2 * kb + 1)
                n = first["loc"] + 2 * kb + 1
                drained(loc_out(act.copy, b, kb, 1), "loc", 2 * kb + 1)
                act.wait_ge(bank_drained[n % NB], n // NB + 1)
                act.sem_inc(sem("loc_ready_act"), 1)
            b = filled(act, "fin")
            copy_signal(fso[:, :], b[0:96, 0:P], "fin", 0, "fso_ready")
            act.wait_ge(sem("fso_ready"), 1)
            for half, t in ((0, new_re), (1, new_im)):
                act.dma_start(t.rearrange("a b d (k g) p -> (a b d k) (g p)", g=2), fso[half * G:(half + 1) * G, :])\
                    .then_inc(sem("state_out"), 16)
            for kb in range(3):
                act.wait_ge(sem("yb_ready"), 2 * kb + 2)
                act.activation(Zg[:, 8 * kb:8 * kb + 8, :], DU[:, 8 * kb:8 * kb + 8, :], ACT.Gelu_apprx_tanh)\
                    .then_inc(sem("z_ready"), 2)
            act.wait_ge(sem("z_ready"), 6)
            act.sem_inc(sem("du_dead"), 6)
            for i in (1, 3, 5):
                b = filled(act, "zc", i)
                copy_signal(zc_view(i), b[0:64, :].rearrange("p (g j h) -> p g j h", j=CH, h=HS), "zc", i, "zc_ready")
            act.wait_ge(sem("state_out"), 32)
            b = filled(act, "zT", 1)
            copy_signal(zT[:, 2:4, :], b.rearrange("p (t x) -> p t x", x=256), "zT", 1, "zT_ready")
            for i in range(3):
                b = filled(act, "glu", i)
                drained(act.activation(ycT[:, 2 * i:2 * i + 2, :], b.rearrange("p (t x) -> p t x", x=256), ACT.Sigmoid),
                        "glu", i)
                n = first["glu"] + i
                act.wait_ge(bank_drained[n % NB], n // NB + 1)
                act.sem_inc(sem("sg_ready"), 1)
            for q in range(4):
                b = filled(act, "g1", q)
                copy_signal(g1s[:, q * MODW:(q + 1) * MODW], b[:, 0:MODW], "g1", q, "g1_ready")
            for tau in range(2):
                act.wait_ge(sem("x2_ready"), 2 * tau + 2)
                act.activation(sqj[:, :], x_tok[:, tau, :], ACT.Square, accum_out=ss[:, tau:tau + 1])\
                    .then_inc(sem("ss_ready"), 1)
                act.wait_ge(sem("ss_ready"), 3 + tau)
            act.wait_ge(sem("ms_ready"), 2)
            act.activation(ss[:, 4:6], ss[:, 2:4], ACT.Sqrt).then_inc(sem("rms_ready"), 1)
            for i in (1, 3):
                b = filled(act, "h2T", i)
                copy_signal(hT[:, 2 * i:2 * i + 2, :], b.rearrange("p (k x) -> p k x", x=256), "h2T", i, "h2T_ready")
            act.wait_ge(sem("lmax_ready"), 1)
            act.activation(ex[:, :, :], eq[0][:, :, :], ACT.Exp).then_inc(sem("ex_ready"), 1)
            act.wait_ge(sem("tables"), 1)
            total = act.value_load(tbl[0:1, 2 * NRT:2 * NRT + 1], min_val=NE, max_val=NR)

            def empty_x(r):
                act.wait_ge(sem("gathered"), r + 1)
                act.copy(Xs[:, :], pX).then_inc(sem("Xs_ready"), 1)

            def empty_sel(r):
                act.wait_ge(sem("sel_turned"), r + 1)
                act.copy(selT[:, :], pX[:, 0:2 * P]).then_inc(sem("selT_ready"), 1)

            act.wait_ge(sem("bias_ready"), 1)
            empty_x(0)
            empty_sel(0)
            with act.Fori(0, total) as R:
                act.wait_ge(sem("gcl_ready"), R + 1)
                act.activation(sgm[:, :], gcl[:, :], ACT.Sigmoid, scale=1.702).then_inc(sem("sgm_ready"), 1)
                empty_x(R + 1)
                act.wait_ge(unit_used[5], R + 1)
                act.copy(ys[:, :], pX).then_inc(sem("ys_ready"), 1)
                empty_sel(R + 1)
            act.wait_ge(sem("end_rows"), 1)
            for q in range(4):
                act.copy(g2s[:, q * MODW:(q + 1) * MODW], ps[:, 4 + q, 0:MODW]).then_inc(sem("g2_ready"), 1)
            for tau in range(2):
                act.wait_ge(sem("x3_ready"), 2 * tau + 2)
                act.activation(sqj[:, :], x_tok[:, tau, :], ACT.Square, accum_out=ss[:, tau:tau + 1])\
                    .then_inc(sem("ss_ready"), 1)
                act.wait_ge(sem("ss_ready"), 5 + tau)
            act.wait_ge(sem("ms_ready"), 3)
            act.activation(ss[:, 4:6], ss[:, 2:4], ACT.Sqrt).then_inc(sem("rms_ready"), 1)
            act.wait_ge(sem("state_out"), 32)

        @block.vector
        def _(dve):
            n_ = [0]

            def link(ins):
                n_[0] += 1
                ins.then_inc(sem("dve_chain"), 1)
                dve.wait_ge(sem("dve_chain"), n_[0])

            def tt(o, a, b_, op):
                link(dve.tensor_tensor(o, a, b_, op))

            def copy_signal(dst, src, stage, i, s):
                drained(dve.tensor_copy(dst, src), stage, i)
                n = first[stage] + i
                dve.wait_ge(bank_drained[n % NB], n // NB + 1)
                dve.sem_inc(sem(s), 1)

            v = lambda i: sc[:, i, :]
            b = filled(dve, "params")
            copy_signal(PT[:, 0:280], b[:, 0:280], "params", 0, "PT_ready")
            lr, li = PT[:, 0:48], PT[:, 48:96]
            link(dve.tensor_scalar(v(0), lr, -1e-4, None, ALU.min))
            dve.wait_ge(sem("dt_ready"), 1)
            tt(v(3), v(0), v(1), ALU.mult)
            dve.sem_inc(sem("er_ready"), 1)
            tt(v(2), li, v(1), ALU.mult)
            link(dve.tensor_scalar(v(5), v(2), 1.0 / TWO_PI, ROUND_MAGIC, ALU.mult, ALU.add))
            link(dve.tensor_scalar(v(5), v(5), -ROUND_MAGIC, None, ALU.add))
            link(dve.scalar_tensor_tensor(out=v(6), in0=v(5), scalar=-C1, in1=v(2), op0=ALU.mult, op1=ALU.add))
            link(dve.scalar_tensor_tensor(out=v(6), in0=v(5), scalar=-C2, in1=v(6), op0=ALU.mult, op1=ALU.add))
            link(dve.scalar_tensor_tensor(out=v(6), in0=v(5), scalar=-C3, in1=v(6), op0=ALU.mult, op1=ALU.add))
            link(dve.tensor_scalar(v(6), v(6), 3.1415925, -3.1415925, ALU.min, ALU.max))
            link(dve.tensor_scalar(v(7), v(6), -1.0, None, ALU.mult))
            tt(v(7), v(7), v(6), ALU.max)
            link(dve.tensor_scalar(v(7), v(7), -1.0, math.pi / 2, ALU.mult, ALU.add))
            dve.sem_inc(sem("angle_ready"), 1)
            tt(v(10), v(0), v(0), ALU.mult)
            tt(v(11), li, li, ALU.mult)
            tt(v(10), v(10), v(11), ALU.add)
            link(dve.reciprocal(v(10), v(10)))
            dve.wait_ge(sem("sig_ready"), 1)
            tt(cs[:, 0:16].rearrange("p (k s) -> p s k", s=2), PT[:, 264:280].rearrange("p (s k) -> p s k", s=2),
               cT[:, :].rearrange("p (s k) -> p s k", s=2), ALU.mult)
            dve.sem_inc(sem("cs_ready"), 1)
            link(dve.memset(Ap[:, 0, 0, :], 1.0))
            link(dve.memset(Ap[:, 1, 0, :], 0.0))
            dve.wait_ge(sem("mag_ready"), 1)
            dve.wait_ge(sem("sin_ready"), 1)
            A = lambda r, m: Ap[:, r, m, :]
            tt(A(0, 1), v(4), v(9), ALU.mult)
            tt(A(1, 1), v(4), v(8), ALU.mult)

            def cmul(ore, oim, ar, ai, br, bi, t):
                tt(ore, ar, br, ALU.mult)
                tt(t, ai, bi, ALU.mult)
                tt(ore, ore, t, ALU.subtract)
                tt(oim, ar, bi, ALU.mult)
                tt(t, ai, br, ALU.mult)
                tt(oim, oim, t, ALU.add)

            cmul(A(0, 2), A(1, 2), A(0, 1), A(1, 1), A(0, 1), A(1, 1), v(5))
            cmul(A(0, 3), A(1, 3), A(0, 2), A(1, 2), A(0, 1), A(1, 1), v(5))
            cmul(A(0, 4), A(1, 4), A(0, 2), A(1, 2), A(0, 2), A(1, 2), v(5))
            dve.sem_inc(sem("powers"), 2)
            link(dve.tensor_scalar(v(12), A(0, 1), -1.0, None, ALU.add))
            tt(v(13), v(12), v(0), ALU.mult)
            tt(v(5), A(1, 1), li, ALU.mult)
            tt(v(13), v(13), v(5), ALU.add)
            tt(v(13), v(13), v(10), ALU.mult)
            tt(v(14), A(1, 1), v(0), ALU.mult)
            tt(v(5), v(12), li, ALU.mult)
            tt(v(14), v(14), v(5), ALU.subtract)
            tt(v(14), v(14), v(10), ALU.mult)
            bc = lambda a: a.unsqueeze(1).broadcast_to([P, CH, G])
            cmul(Fp[:, 0], Fp[:, 1], bc(v(13)), bc(v(14)), Ap[:, 0, 0:CH, :], Ap[:, 1, 0:CH, :], sc[:, 5:9, :])
            link(dve.tensor_copy(a4r[:, :], A(0, 4)))
            link(dve.tensor_copy(a4i[:, 1, :], A(1, 4)))
            link(dve.tensor_scalar(a4i[:, 0, :], A(1, 4), -1.0, None, ALU.mult))
            link(dve.tensor_copy(dcol[:, :], PT[:, 240:264]))
            for i in range(4):
                b = filled(dve, "B", i)
                ins = dve.tensor_copy(Bt[:, 4 * i:4 * i + 4, :], b[:, 0:384].rearrange("p (h x) -> p h x", x=96))
                drained(ins, "B", i)
            n = first["B"] + 3
            dve.wait_ge(bank_drained[n % NB], n // NB + 1)

            def bbx_fill(d):
                j0 = CH - 1 if d == 0 else 0
                if d == 0:
                    dve.wait_ge(sem("cleared"), 4)
                else:
                    dve.wait_ge(bank_full, first["gt0"] + 6)
                    link(dve.memset(bbx[1][:, :, :, :, :], 0.0))
                for g2 in range(2):
                    rows = slice(64 * g2, 64 * g2 + 64)
                    for r in range(2):
                        link(dve.tensor_copy(bbx[d][rows, :, r, g2, :].rearrange("p k h -> p h k"), gm[d][rows, r, j0, :, :]))
                dve.sem_inc(sem("bbx_ready"), 1)

            for d in range(2):
                step = slice(None, None, -1) if d == 0 else slice(None)
                wr, wi = (Fp[:, r, step, d * NP:(d + 1) * NP].unsqueeze(2).broadcast_to([P, CH, HS, NP]) for r in range(2))
                br, bi = (Bt[:, :, r * G + d * NP:r * G + (d + 1) * NP].unsqueeze(1).broadcast_to([P, CH, HS, NP])
                          for r in range(2))
                cmul(gm[d][:, 0], gm[d][:, 1], wr, wi, br, bi, tmpg[:, :, :, :])
                dve.sem_inc(sem("gm_ready"), 1)
                bbx_fill(d)

            def norm_scale(nth):
                dve.wait_ge(sem("ss_ready"), 2 * nth)
                link(dve.tensor_scalar(ss[:, 2:4], ss[:, 0:2], 1.0 / D, EPS, ALU.mult, ALU.add))
                dve.sem_inc(sem("ms_ready"), 1)
                dve.wait_ge(sem("rms_ready"), nth)
                link(dve.reciprocal(ss[:, 6:8], ss[:, 4:6]))

            def mod_rows(j, gain=None):
                dve.wait_ge(sem("mod_filled"), 2 * (j // 2) + 2)
                m = mod[:, j * MODW:(j + 1) * MODW]
                tt(m, ps[:, 5 + j // 2, (j % 2) * MODW:(j % 2 + 1) * MODW], m, ALU.add)
                if gain is not None:
                    link(dve.scalar_tensor_tensor(out=m, in0=m, scalar=1.0, in1=gains[:, gain, :], op0=ALU.add, op1=ALU.mult))
                dve.sem_inc(sem("mod_rows"), 1)

            def modulate(dst, s_gs, s_sh, ready):
                for q in range(4):
                    b = filled(dve, s_gs, q)
                    for tau in range(2):
                        ins = dve.scalar_tensor_tensor(out=dst[:, tau, q * MODW:(q + 1) * MODW],
                                                       in0=x_tok[:, tau, q * MODW:(q + 1) * MODW],
                                                       scalar=ss[:, 6 + tau:7 + tau], in1=b[:, 0:MODW],
                                                       op0=ALU.mult, op1=ALU.mult)
                    drained(ins, s_gs, q)
                n = first[s_gs] + 3
                dve.wait_ge(bank_drained[n % NB], n // NB + 1)
                for q in range(4):
                    b = filled(dve, s_sh, q)
                    for tau in range(2):
                        h = dst[:, tau, q * MODW:(q + 1) * MODW]
                        link(dve.tensor_tensor(h, h, b[:, 0:MODW], ALU.add))
                        dve.sem_inc(sem(ready), 1)
                    dve.sem_inc(bank_drained[(first[s_sh] + q) % NB], 1)

            norm_scale(1)
            dve.wait_ge(sem("rows_in"), 16 * 16)
            mod_rows(0)
            mod_rows(1, 0)
            dve.sem_inc(sem("gain_dead"), 1)
            b = filled(dve, "m12")
            copy_signal(cst[:, _C["ccbd"][0]:_C["ccbd"][0] + 512], b, "m12", 0, "m12_ready")
            modulate(h_tok, "gs1", "sh1", "h_ready")
            for i in (0, 2):
                b = filled(dve, "hT", i)
                copy_signal(hT[:, 2 * i:2 * i + 2, :], b.rearrange("p (k x) -> p k x", x=256), "hT", i, "hT_ready")
            dve.wait_ge(bank_full, first["hT"] + 4)
            link(dve.tensor_copy(ist[:, :, :], PT[:, 96:192].rearrange("p (r k) -> p r k", r=2)))
            dve.wait_ge(sem("ca_ready"), 2)
            dve.sem_inc(sem("uc_free"), 1)
            dve.sem_inc(sem("scratch_dead"), 1)
            for i in range(4):
                b = filled(dve, "u", i)
                tau, n = i // 2, i % 2
                link(dve.tensor_copy(uc[:, 24 * n:24 * n + 24, :, 2 * tau, :], twice(b[0:64, 0:384])))
                dve.sem_inc(sem("uc_ready_dve"), 1)
                dve.wait_ge(sem("uc_ready_act"), i + 1)
                dve.sem_inc(bank_drained[(first["u"] + i) % NB], 1)
            b = filled(dve, "K0").rearrange("p (b x) -> p b x", x=64)[:, 0:6, :]
            drained(dve.tensor_copy(KK[:, :, 48:112], b), "K0")
            n = first["K0"]
            dve.wait_ge(bank_drained[n % NB], n // NB + 1)
            dve.sem_inc(sem("windows"), 1)
            b = filled(dve, "K1").rearrange("p (b x) -> p b x", x=64)[:, 0:6, :]
            dve.tensor_copy(KK[:, :, 0:48], b[:, :, 0:48])
            drained(dve.tensor_tensor(KK[:, :, 48:64], KK[:, :, 48:64], b[:, :, 48:64], ALU.add), "K1")
            n = first["K1"]
            dve.wait_ge(bank_drained[n % NB], n // NB + 1)
            dve.sem_inc(sem("windows"), 1)
            for i in (0, 2, 4):
                b = filled(dve, "U", i)
                copy_signal(U[:, 8 * i:8 * i + 8, :], b.rearrange("p (g x) -> p g x", x=TC), "U", i, "U_ready")
            for kb in range(6):
                b = filled(dve, "loc", 2 * kb)
                n = first["loc"] + 2 * kb
                drained(loc_out(dve.tensor_copy, b, kb, 0), "loc", 2 * kb)
                dve.wait_ge(bank_drained[n % NB], n // NB + 1)
                dve.sem_inc(sem("loc_ready_dve"), 1)
            link(dve.memset(SL[:, :, 0, 0, :], 0.0))
            link(dve.memset(SL[:, :, 1, NC, :], 0.0))
            link(dve.tensor_copy(SL[:, :, 0, 0, 1::2], ist[:, :, 0:NP]))
            link(dve.tensor_copy(SL[:, :, 1, NC, 1::2], ist[:, :, NP:G]))
            dve.sem_inc(sem("init_ready"), 1)
            dve.wait_ge(sem("loc_ready_act"), 6)
            scan(dve, link, 0)
            dve.sem_inc(sem("scan_dve"), 1)
            link(dve.tensor_copy(fs[:, :, 0:NP], SL[:, :, 0, NC, 0::2]))
            for j in range(2, 6):
                mod_rows(j, 1 if j == 4 else None)
            dve.wait_ge(sem("scan_pool"), 1)
            link(dve.tensor_copy(fs[:, :, NP:G], SL[:, :, 1, 0, 0::2]))
            dve.sem_inc(sem("fs_ready"), 1)
            dve.wait_ge(sem("du_ready"), 2)
            for kb in range(3):
                for g2 in range(2):
                    rows = slice(64 * g2, 64 * g2 + 64)
                    b = filled(dve, "y", 2 * kb + g2)
                    y = DU[rows, 8 * kb:8 * kb + 8, :]
                    drained(dve.tensor_tensor(y, y, b[rows, :].rearrange("p (k x) -> p k x", x=TC), ALU.add),
                            "y", 2 * kb + g2)
                    n = first["y"] + 2 * kb + g2
                    dve.wait_ge(bank_drained[n % NB], n // NB + 1)
                    dve.sem_inc(sem("yb_ready"), 1)
            for i in (0, 2, 4):
                b = filled(dve, "zc", i)
                copy_signal(zc_view(i), b[0:64, :].rearrange("p (g j h) -> p g j h", j=CH, h=HS), "zc", i, "zc_ready")
            dve.wait_ge(sem("state_out"), 32)
            for i in (0, 2):
                b = filled(dve, "zT", i)
                copy_signal(zT[:, 2 * i:2 * i + 2, :], b.rearrange("p (t x) -> p t x", x=256), "zT", i, "zT_ready")
            for i in range(3):
                dve.wait_ge(sem("sg_ready"), i + 1)
                dve.wait_ge(sem("zT_ready"), 3)
                y = ycT[:, 2 * i:2 * i + 2, :]
                tt(y, y, zT[:, 2 * i:2 * i + 2, :], ALU.mult)
                dve.sem_inc(sem("yc_ready"), 1)
            dve.wait_ge(sem("g1_ready"), 4)
            for tau in range(2):
                for dh in range(2):
                    i = 2 * tau + dh
                    b = filled(dve, "o", i)
                    tt(otmp[:, :], b, g1s[:, dh * HALF:(dh + 1) * HALF], ALU.mult)
                    dve.sem_inc(bank_drained[(first["o"] + i) % NB], 1)
                    x = x_tok[:, tau, dh * HALF:(dh + 1) * HALF]
                    tt(x, x, otmp[:, :], ALU.add)
                    dve.sem_inc(sem("x2_ready"), 1)
            norm_scale(2)
            modulate(h2, "gs2", "sh2", "h2_ready")
            for i in (0, 2):
                b = filled(dve, "h2T", i)
                copy_signal(hT[:, 2 * i:2 * i + 2, :], b.rearrange("p (k x) -> p k x", x=256), "h2T", i, "h2T_ready")
            b = filled(dve, "lg")
            link(dve.tensor_copy(lg[:, :, :], b[:, 0:2 * NE].rearrange("p (t e) -> p t e", e=NE)))
            dve.sem_inc(bank_drained[first["lg"] % NB], 1)
            for tau in range(2):
                link(dve.max(m8[:, tau, :], lg[:, tau, :]))
            wide = lambda a: a.broadcast_to([P, 2, NE])
            fourth = wide(m8[:, :, 3:4])
            tt(eq[0][:, :, :], lg[:, :, :], wide(m8[:, :, 0:1]), ALU.subtract)
            dve.sem_inc(sem("lmax_ready"), 1)
            tt(gt[:, :, :], lg[:, :, :], fourth, ALU.is_gt)
            dve.wait_ge(sem("ex_ready"), 1)
            tt(rank[:, :, :], lg[:, :, :], fourth, ALU.is_equal)
            link(dve.tensor_copy(eq[0][:, :, :], rank[:, :, :]))
            a_, b_ = eq
            for sft in (1, 2, 4, 8, 16):
                dve.tensor_copy(b_[:, :, 0:sft], a_[:, :, 0:sft])
                tt(b_[:, :, sft:NE], a_[:, :, sft:NE], a_[:, :, 0:NE - sft], ALU.add)
                a_, b_ = b_, a_
            link(dve.tensor_reduce(r1c[:, 0:2], gt[:, :, :], AX.X, ALU.add))
            tt(a_[:, :, :], a_[:, :, :], wide(r1c[:, 0:2].unsqueeze(2)), ALU.add)
            link(dve.scalar_tensor_tensor(out=a_[:, :, :], in0=a_[:, :, :], scalar=4.0, in1=rank[:, :, :],
                                          op0=ALU.is_le, op1=ALU.mult))
            tt(gt[:, :, :], gt[:, :, :], a_[:, :, :], ALU.add)
            dve.sem_inc(sem("mask_ready"), 1)
            tt(ex[:, :, :], ex[:, :, :], gt[:, :, :], ALU.mult)
            link(dve.tensor_reduce(r1c[:, 4:6], ex[:, :, :], AX.X, ALU.add))
            link(dve.reciprocal(r1c[:, 6:8], r1c[:, 4:6]))
            tt(comb[:, :, :], ex[:, :, :], wide(r1c[:, 6:8].unsqueeze(2)), ALU.mult)
            dve.sem_inc(sem("comb_ready"), 1)
            b = filled(dve, "rk")
            link(dve.tensor_copy(cnt[:, 0:1], b[0:NE, 64:65]))
            link(dve.scalar_tensor_tensor(out=rank[:, :, :], in0=b[:, 0:2 * NE].rearrange("p (t e) -> p t e", e=NE),
                                          scalar=1.0, in1=gt[:, :, :], op0=ALU.add, op1=ALU.mult))
            dve.sem_inc(bank_drained[first["rk"] % NB], 1)
            link(dve.tensor_scalar(rank[:, :, :], rank[:, :, :], -1.0, None, ALU.add))
            link(dve.tensor_scalar(cnt[:, 1:2], cnt[:, 0:1], float(SL_), 1.0, ALU.is_gt, ALU.add))
            for n in range(2, 2 * L // SL_):
                link(dve.scalar_tensor_tensor(out=cnt[:, 1:2], in0=cnt[:, 0:1], scalar=float(n * SL_), in1=cnt[:, 1:2],
                                              op0=ALU.is_gt, op1=ALU.add))
            dve.sem_inc(sem("rounds_ready"), 1)
            b = filled(dve, "cu")
            tt(cnt[:, 4:5], b[0:NE, 0:1], cnt[:, 1:2], ALU.add)
            dve.sem_inc(bank_drained[first["cu"] % NB], 1)
            link(dve.tensor_scalar(cmp[:, 0:NRT], C("iota", slice(0, NE))[:, 0:NRT], cnt[:, 4:5], None, ALU.is_ge))
            dve.sem_inc(sem("cmp_ready"), 1)
            b = filled(dve, "tb")
            link(dve.tensor_scalar(tbl[:, 0:NRT], b[0:1, 0:NRT], float(NE - 1), None, ALU.min))
            tt(brt_f[:, 0:NRT], C("iota", slice(0, 1))[:, 0:NRT], b[0:1, NRT:2 * NRT], ALU.subtract)
            link(dve.tensor_scalar(tbl[:, NRT:2 * NRT], brt_f[:, 0:NRT], float(SL_), None, ALU.mult))
            link(dve.tensor_copy(tbl[:, 2 * NRT:2 * NRT + 1 + NE], b[0:1, 2 * NRT:2 * NRT + 1 + NE]))
            dve.sem_inc(bank_drained[first["tb"] % NB], 1)
            dve.sem_inc(sem("tables"), 1)
            b = filled(dve, "cb")
            link(dve.tensor_copy(combT[:, :], b[0:NE, 0:256]))
            dve.sem_inc(bank_drained[first["cb"] % NB], 1)
            dve.sem_inc(sem("combT_ready"), 1)
            total = dve.value_load(tbl[0:1, 2 * NRT:2 * NRT + 1], min_val=NE, max_val=NR)

            def select(r):
                e = dve.value_load(tbl[0:1, bass.ds(r, 1)], min_val=0, max_val=NE - 1)
                base = dve.value_load(tbl[0:1, bass.ds(r + NRT, 1)], min_val=0, max_val=256 - SL_)
                lo = _C["iota"][0]
                slots = cst[:, bass.ds(base + lo, SL_)]
                for tau in range(2):
                    dve.tensor_scalar(sel[:, tau, :], slots, rank[:, tau, bass.ds(e, 1)], None, ALU.is_equal)
                    for n in range(2):
                        ins = dve.tensor_scalar(selw[:, tau, n, :], slots, rank[:, tau, bass.ds(e, 1)],
                                                comb[:, tau, bass.ds(e, 1)], ALU.is_equal, ALU.mult)
                ins.then_inc(sem("sel_ready"), 1)
                return e

            def bias_row(e):
                dve.tensor_copy(selb[:, :], cst[0:96, bass.ds(e + _C["eye"][0], 1)].broadcast_to([96, SL_]))\
                    .then_inc(sem("selb_ready"), 1)

            dve.wait_ge(sem("bias_ready"), 1)
            bias_row(select(0))
            dve.wait_ge(sem("X_turned"), 1)
            dve.tensor_copy(XT[:, :, :], pT.rearrange("p (n x) -> p n x", x=P)).then_inc(sem("XT_ready"), 1)
            with dve.Fori(0, total) as R:
                dve.wait_ge(sem("gathered"), R + 1)
                dve.wait_ge(sem("sel_turned"), R + 1)
                e1 = select(R + 1)
                dve.wait_ge(unit_used[1], R + 1)
                dve.tensor_scalar(gcl[:, :], pG, 7.0, None, ALU.min).then_inc(sem("gcl_ready"), 1)
                dve.wait_ge(unit_used[3], R + 1)
                dve.tensor_scalar(upc[:, :], pU, 7.0, -7.0, ALU.min, ALU.max).then_inc(sem("upc_ready"), 1)
                bias_row(e1)
                dve.wait_ge(sem("upc_ready"), R + 1)
                dve.wait_ge(sem("gcl_ready"), R + 1)
                dve.scalar_tensor_tensor(out=upc[:, :], in0=upc[:, :], scalar=1.0, in1=gcl[:, :], op0=ALU.add,
                                         op1=ALU.mult).then_inc(sem("glin_ready"), 1)
                dve.wait_ge(sem("glin_ready"), R + 1)
                dve.wait_ge(sem("sgm_ready"), R + 1)
                dve.tensor_tensor(acts[:, :], upc[:, :], sgm[:, :], ALU.mult).then_inc(sem("act_ready"), 1)
                dve.wait_ge(sem("X_turned"), R + 2)
                dve.tensor_copy(XT[:, :, :], pT.rearrange("p (n x) -> p n x", x=P)).then_inc(sem("XT_ready"), 1)
                dve.wait_ge(sem("act_turned"), R + 1)
                dve.tensor_copy(actT[:, :, :], pT.rearrange("p (n x) -> p n x", x=P)).then_inc(sem("actT_ready"), 1)
            dve.wait_ge(sem("scattered"), total)
            dve.wait_ge(sem("gathered"), total + 1)
            dve.wait_ge(sem("g2_ready"), 4)
            for tau in range(2):
                for dh in range(2):
                    tt(Xs[:, :], OUT[tau][dh], g2s[:, dh * HALF:(dh + 1) * HALF], ALU.mult)
                    x = x_tok[:, tau, dh * HALF:(dh + 1) * HALF]
                    tt(x, x, Xs[:, :], ALU.add)
                    dve.sem_inc(sem("x3_ready"), 1)
            norm_scale(3)
            for tau in range(2):
                for q in range(4):
                    link(dve.scalar_tensor_tensor(out=h2[:, tau, q * MODW:(q + 1) * MODW],
                                                  in0=x_tok[:, tau, q * MODW:(q + 1) * MODW],
                                                  scalar=ss[:, 6 + tau:7 + tau], in1=ps[:, 4 + q, MODW:2 * MODW],
                                                  op0=ALU.mult, op1=ALU.mult))
                dve.sem_inc(sem("y_ready"), 1)


_INS = ['x_prompt', 'x_sample', 'c', 'state_s5_re', 'state_s5_im', 'c_ctx', 'w_ada', 'b_ada', 'norm1_g', 'w_in',
        's5_lam_re', 's5_lam_im', 's5_log_dt', 's5_b_re', 's5_b_im', 's5_c_re', 's5_c_im', 's5_d', 's5_w_glu',
        'w_fnet', 'w_out', 'norm2_g', 'w_router', 'b_router', 'w_gate', 'b_gate', 'w_up', 'b_up', 'w_down',
        'b_down', 'norm_f_g']
_OUTS = [(1, L, D), (1, L, D), (1, 1, 2, G, ST), (1, 1, 2, G, ST)]


def kernel(**inputs):
    import concourse.bacc as bacc
    from concourse.bass_utils import run_bass_kernel_spmd

    nc = bacc.Bacc("TRN2", target_bir_lowering=False, num_devices=1)
    arrays, args = {}, []
    for name, a in [("constants", constant_tile()), ("positions", position_table())] + \
            [(n, inputs[n]) for n in _INS]:
        a = np.ascontiguousarray(a)
        arrays[f"in_{name}"] = a
        args.append(nc.dram_tensor(f"in_{name}", a.shape, mybir.dt.from_np(a.dtype), kind="ExternalInput").ap())
    for i, shape in enumerate(_OUTS):
        args.append(nc.dram_tensor(f"out_{i}", shape, F32, kind="ExternalOutput").ap())
    build(nc, *args)
    r = run_bass_kernel_spmd(nc, [arrays], core_ids=[0])
    return tuple(r.results[0][f"out_{i}"] for i in range(len(_OUTS)))
```

```python
import math
from contextlib import ExitStack

import numpy as np

import concourse.bass as bass
from concourse import mybir

F32 = mybir.dt.float32
BF16 = mybir.dt.bfloat16
I32 = mybir.dt.int32
ALU = mybir.AluOpType
ACT = mybir.ActivationFunctionType
AX = mybir.AxisListType

P = 128
D = 1024
L = 128
KD = D // P
CH = 4
NC = L // CH
G = 48
NP = G // 2
HS = 16
ST = 64
DS5 = G * HS
NCT = DS5 // P
TC = 2 * NC
NE = 32
SL_ = 64
NR = NE + 4 * 2 * L // SL_
NRT = NR + 1
HALF = 512
MODW = 256
SPLIT = 8
EPS = 1e-6
TWO_PI = 2.0 * math.pi
C1 = 6.28125
C2 = float(np.float32(np.round((TWO_PI - C1) * 2.0 ** 20) / 2.0 ** 20))
C3 = TWO_PI - C1 - C2
ROUND_MAGIC = 1.5 * 2.0 ** 23

NSLOT = 8
K_ROWS = KD


def pair_slot(e, m):
    return (3 * e + m) % (NSLOT // 2)


_C = {}
_w = 0
for _n, _k in (("ident", P), ("ones", P), ("ssel", P), ("triu", P), ("cosL", P), ("sinL", P),
               ("ccbd", P), ("nscbd", P), ("wfbd", 2 * P), ("iota", 256), ("eye", NE)):
    _C[_n] = (_w, _w + _k)
    _w += _k
CW = _w


def constant_tile():
    t = np.zeros((P, CW), np.float32)

    def put(name, a):
        t[:a.shape[0], _C[name][0]:_C[name][0] + a.shape[1]] = a

    put("ident", np.eye(P))
    put("ones", np.ones((P, P)))
    ssel = np.zeros((P, P))
    tok_stream = (np.arange(P) // NC) % 2
    for q in range(4):
        for s in range(2):
            ssel[32 * q + s] = tok_stream == s
    put("ssel", ssel)
    put("triu", np.triu(np.ones((P, P)), 1))
    r = np.arange(P)
    tt = CH * (r % NC) + r // NC
    ang = 2 * np.pi * np.outer(tt, tt) / L
    norm = 1.0 / np.sqrt(L * 64.0)
    put("cosL", np.cos(ang) * norm)
    put("sinL", np.sin(ang) * norm)
    ca = 2 * np.pi * np.outer(np.arange(64), np.arange(64)) / 64
    put("ccbd", np.kron(np.eye(2), np.cos(ca)))
    put("nscbd", -np.kron(np.eye(2), np.sin(ca)))
    put("iota", np.tile(np.arange(256.0), (P, 1)))
    put("eye", np.tile(np.eye(NE), (4, 1)))
    return t


def position_table():
    t = np.arange(L)
    q = D // 4
    omega = (np.float32(1.0) / np.float32(10000.0) ** (np.arange(q, dtype=np.float32) / np.float32(q))).astype(np.float32)

    def emb(p):
        a = p.astype(np.float32)[:, None] * omega[None]
        return np.concatenate([np.sin(a), np.cos(a)], -1)

    return np.concatenate([emb(t // 64), emb(t % 64)], -1).astype(np.float32)


def build(nc, cst_d, pos_d, x_prompt, x_sample, c_lat, st_re, st_im, c_ctx, w_ada, b_ada, norm1_g, w_in,
          lam_re, lam_im, log_dt, b_re, b_im, c_re, c_im, d_skip, w_glu, w_fnet, w_out, norm2_g,
          w_router, b_router, w_gate, b_gate, w_up, b_up, w_down, b_down, norm_f_g,
          y_prompt, y_sample, new_re, new_im):
    ctx = ExitStack()
    with ctx:
        BASE = 16512
        SLOT = 4 * D * 4
        RING = BASE
        E_OFF = RING + 3 * SLOT
        W_OFF = RING + 6 * SLOT
        R_OFF = W_OFF + 8 * D * 4
        top = [0]

        def at(name, off, shape, dt=F32):
            n = int(np.prod(shape[1:])) * (2 if dt == BF16 else 4)
            top[0] = max(top[0], off + n)
            return nc.alloc_sbuf_tensor_at(name, shape, dt, offset=off)

        ring = [at(f"ring{i}", RING + i * SLOT, [P, 4, D]) for i in range(NSLOT)]
        natB = at("natB", RING, [96, 2 * ST, HS])
        natC = at("natC", RING + 8192, [96, HS, 2, ST])
        ca = at("ca", E_OFF, [P, 2, 2, 5, HS, NP])
        U = at("U", E_OFF + 30720, [P, G, TC])
        DU = at("DU", E_OFF + 30720 + 12288, [P, NP, TC])
        gm = [at(f"gm{d}", E_OFF + 30720 + d * 12288, [P, 2, CH, HS, NP]) for d in range(2)]
        Bt = at("Bt", W_OFF + 6144, [P, HS, 96])
        Ct = at("Ct", W_OFF + 12288, [P, HS, 96])
        h_tok = at("h_tok", W_OFF + 18432, [P, 2, D])
        bbx = [at(f"bbx{d}", (W_OFF + 26624, E_OFF + 30720)[d], [P, NP, 2, 2, HS]) for d in range(2)]
        uc = at("uc", W_OFF, [64, G, 2, CH, HS])
        SL = at("SL", W_OFF, [P, 2, 2, NC + 1, G])
        ufT = at("ufT", W_OFF + 26624, [P, 2, 2, L])
        Zs = at("Zs", W_OFF + 28672, [P, 2, 2, 256])
        wout = at("wout", W_OFF, [P, KD, D])
        GT = at("GT", R_OFF, [P, G, P])
        Zg = at("Zg", R_OFF, [P, NP, TC])
        zc = at("zc", R_OFF + 6144, [64, CH, DS5])
        zT = at("zT", R_OFF + 18432, [P, NCT, 256])
        g1s = at("g1s", R_OFF + 6144, [P, D])
        h2 = at("h2", R_OFF, [P, 2, D])
        bdn = at("bdn", R_OFF + 8192, [NE, D])
        braw = at("braw", R_OFF + 12288, [96, 2, D])
        MISC = R_OFF + 20480
        T_OFF = R_OFF + 24576
        T = at("T", T_OFF, [P, NP, CH * HS])
        bias3 = at("bias3", T_OFF, [96, 2, D], BF16)
        wrt = at("wrt", T_OFF + 4096, [P, KD, NE])
        G_OFF = T_OFF + 6144
        tmpg = at("tmpg", G_OFF, [P, CH, HS, NP])
        KK = at("KK", G_OFF, [P, 6, 7 * HS])
        tmpc = at("tmpc", G_OFF + 6144, [P, 5, HS, NP])
        SM = G_OFF + 6144 + 7680
        wglu = at("wglu", G_OFF, [P, NCT, DS5])
        X_OFF = G_OFF + 18432
        x_tok = at("x_tok", X_OFF, [P, 2, D])
        mod = at("mod", X_OFF + 8192, [P, 6 * MODW])
        HT_OFF = X_OFF + 8192 + 6144
        hT = at("hT", HT_OFF, [P, KD, 256])
        ycT = at("ycT", HT_OFF, [P, KD, 256])
        CO = HT_OFF + 8192
        cst = at("cst", CO, [P, CW])
        CO2 = CO + CW * 4
        gains = at("gains", CO2, [P, 2, MODW])
        cs = at("cs", CO2 + 2048, [P, 46])
        a4r = at("a4r", CO2 + 2048 + 192, [P, G])
        a4i = at("a4i", CO2 + 2048 + 384, [P, 2, G])
        dcol = at("dcol", CO2 + 2048 + 768, [P, NP])
        ss = at("ss", CO2 + 2048 + 864, [P, 8])
        scan_q = at("scan_q", CO2 + 2048 + 896, [P, 2, 2, G])
        scan_p = at("scan_p", W_OFF + 25344, [P, 2, 2, G])
        ist = at("ist", W_OFF + 25344 + 768, [P, 2, G])
        fs = at("fs", R_OFF + 18432, [P, 2, G])
        fso = at("fso", R_OFF + 18432 + 512, [96, P])
        sqj = at("sqj", R_OFF + 12288, [P, D])
        otmp = at("otmp", R_OFF + 10240, [P, HALF])
        g2s = at("g2s", HT_OFF, [P, D])
        gfs = at("gfs", HT_OFF + 4096, [P, D])
        assert top[0] <= 229344, top[0]

        def C(name, rows=slice(None)):
            a, b = _C[name]
            return cst[rows, a:b]

        PT = at("PT", SM, [P, 288])
        natL = at("natL", T_OFF, [96, P])
        natS = at("natS", T_OFF + 512, [96, P])
        natT = at("natT", T_OFF + 1024, [G, 2, ST])
        natD = at("natD", T_OFF + 1536, [NP, 2, CH, HS])
        natCc = at("natCc", T_OFF + 2048, [16, P])
        rawT = at("rawT", T_OFF + 2560, [G, 2])
        rawD = at("rawD", T_OFF + 2592, [NP, 2, HS])
        Ap = at("Ap", SM + 1152, [P, 2, 5, G])
        Fp = at("Fp", SM + 1152 + 1920, [P, 2, CH, G])
        sc = at("sc", T_OFF + 2752, [P, 16, G])
        cT = at("cT", T_OFF + 2752 + 3072, [P, 16])

        Xs = at("Xs", G_OFF, [P, HALF])
        XT = at("XT", G_OFF + 2048, [P, 4, P])
        gcl = at("gcl", G_OFF + 4096, [P, HALF])
        sgm = at("sgm", G_OFF + 6144, [P, HALF])
        upc = at("upc", G_OFF + 8192, [P, HALF])
        acts = at("acts", G_OFF + 10240, [P, HALF])
        actT = at("actT", G_OFF + 12288, [P, 4, P])
        ys = at("ys", G_OFF + 14336, [P, HALF])
        sel = at("sel", G_OFF + 16384, [P, 2, SL_])
        selw = at("selw", G_OFF + 16384 + 512, [P, 2, 2, SL_])
        selb = at("selb", G_OFF + 16384 + 1536, [96, SL_], BF16)
        selT = at("selT", T_OFF + 5120, [P, 2 * P])
        lg = at("lg", MISC, [P, 2, NE])
        m8 = at("m8", MISC + 256, [P, 2, 8])
        gt = at("gt", MISC + 320, [P, 2, NE])
        eq = [at(f"eq{i}", MISC + 576 + 256 * i, [P, 2, NE]) for i in range(2)]
        ex = at("ex", MISC + 1088, [P, 2, NE])
        rank = at("rank", MISC + 1344, [P, 2, NE])
        comb = at("comb", MISC + 1600, [P, 2, NE])
        r1c = at("r1c", MISC + 1856, [P, 8])
        cnt = at("cnt", MISC + 1888, [NE, 8])
        cmp = at("cmp", MISC + 1920, [NE, 52])
        brt_f = at("brt_f", MISC + 2944, [1, 64])
        tbl = at("tbl", MISC + 2144, [1, 160], I32)
        brt = at("brt", MISC + 2784, [1, NE])
        combT = at("combT", T_OFF + 5120, [NE, 256])
        r1 = at("r1", G_OFF + 4096, [96, 2, D])

        ps = ctx.enter_context(nc.psum_tensor("ps", [P, 8, HALF], F32))
        kd_dram = nc.dram_tensor("k_windows", [G * HS, 7 * HS], F32, kind="Internal").ap()

        S = {}

        def sem(name):
            if name not in S:
                S[name] = ctx.enter_context(nc.semaphore(name))
            return S[name]

        NB = 5
        STAGES = (("params", 1), ("B", 4), ("Cc", 4), ("gt0", 6), ("gt1", 6), ("m12", 1),
                  ("gs1", 4), ("sh1", 4), ("K0", 1), ("hT", 4), ("u", 4), ("K1", 1), ("U", 6), ("loc", 12), ("uf", 1),
                  ("Z", 2), ("yf", 1), ("y0", 2), ("y1", 2), ("fin", 1), ("y2", 2), ("zc", 6), ("zT", 3), ("glu", 3), ("g1", 4), ("o", 4),
                  ("gs2", 4), ("sh2", 4), ("h2T", 4), ("lg", 1), ("end", 4), ("rk", 1), ("cu", 1), ("tb", 1), ("cb", 1))
        first = {}
        njobs = 0
        for n_, k_ in STAGES:
            first[n_] = njobs
            njobs += k_
        bank_full = sem("bank_full")
        bank_drained = [sem(f"bank_drained{b}") for b in range(NB)]

        def bank(stage, i=0):
            return ps[:, (first[stage] + i) % NB, :]

        def claim(pe, stage, i=0):
            n = first[stage] + i
            if n >= NB:
                pe.wait_ge(bank_drained[n % NB], n // NB)
            return ps[:, n % NB, :]

        def filled(eng, stage, i=0):
            eng.wait_ge(bank_full, first[stage] + i + 1)
            return ps[:, (first[stage] + i) % NB, :]

        def drained(ins, stage, i=0):
            ins.then_inc(bank_drained[(first[stage] + i) % NB], 1)

        OUT = [[ps[:, 2 * tau + dh, :] for dh in range(2)] for tau in range(2)]
        pG, pU, pX, pT = (ps[:, b, :] for b in (4, 5, 6, 7))

        early = [("ada", 0, 0), ("ada", 0, 1), ("ada", 1, 0), ("ada", 1, 1), ("w_in", 0, 0), ("w_in", 0, 1)]
        early += [("ada", j, b) for j in range(2, 6) for b in range(2)]
        early_id = {u: n + 1 for n, u in enumerate(early)}
        early_in = [sem(f"early_in{i}") for i in range(3)]
        early_used = [sem(f"early_used{i}") for i in range(3)]

        def early_wait(eng, unit):
            n = early_id[unit]
            eng.wait_ge(early_in[n % 3], 16 * (n // 3 + (1 if n % 3 else 2)))
            return ring[n % 3]

        def early_release(ins, unit):
            ins.then_inc(early_used[early_id[unit] % 3], 1)

        def mod_bank(j):
            col = (j % 2) * MODW
            return ps[:, 5 if j == 5 else 5 + j // 2, col:col + MODW]

        block = ctx.enter_context(nc.Block())

        def tok_rows(j, s):
            b = (j % 2) * 64 + s * 32
            return slice(b, b + 32), j // 2

        def store_tokens(eng, j):
            for s, t in ((0, y_prompt), (1, y_sample)):
                rows, tau = tok_rows(j, s)
                eng.dma_start(t[0].rearrange("(c j) d -> j c d", j=CH)[j], h2[rows, tau, :]).then_inc(sem("y_out"), 16)

        W6 = [(w_gate, 0), (w_gate, 1), (w_up, 0), (w_up, 1), (w_down, 0), (w_down, 1)]
        UNITS = ("g0", "g1", "u0", "u1", "d0", "d1")
        unit_in = [sem(f"expert_{u}_in") for u in UNITS]
        unit_used = [sem(f"expert_{u}_used") for u in UNITS]

        def halves(w, e, b):
            return w[0, e].rearrange("(b k p) c -> b p k c", b=2, p=P)[b]

        @block.sync
        def _(sp):
            def load(dst, src, s):
                sp.dma_start(dst, src).then_inc(sem(s), 16)

            load(cst[:, :], cst_d, "cst_in")
            for half, t in ((0, lam_re), (1, lam_im)):
                load(natL[half * G:(half + 1) * G, :], t.rearrange("a d (k g) p -> (a d k) (g p)", g=2), "small_in")
            for half, t in ((0, st_re), (1, st_im)):
                load(natS[half * G:(half + 1) * G, :], t.rearrange("a b d (k g) p -> (a b d k) (g p)", g=2), "small_in")
            load(rawT[:, :], log_dt.rearrange("a d (k g) -> (a d k) g", g=2), "small_in")
            load(rawD[:, :, :], d_skip.rearrange("a (k g h) -> (a k) g h", g=2, h=HS), "small_in")
            load(natCc[0:8, :], c_ctx.rearrange("(k p) -> k p", p=P), "small_in")
            load(natCc[8:16, :], c_lat.rearrange("a (k p) -> (a k) p", p=P), "small_in")
            for half, t in ((0, b_re), (1, b_im)):
                sp.dma_start(natB[half * G:(half + 1) * G, :, :],
                             t.rearrange("a d (k g) p h -> (a d k) (g p) h", g=2)).then_inc(early_in[0], 16)
            for half, t in ((0, c_re), (1, c_im)):
                for g2 in range(2):
                    sp.dma_start(natC[half * G:(half + 1) * G, :, g2, :],
                                 t.rearrange("a d (k g) h p -> g (a d k) h p", g=2)[g2]).then_inc(sem("natC_in"), 16)
            for j in range(CH):
                for s, t in ((0, x_prompt), (1, x_sample)):
                    rows, tau = tok_rows(j, s)
                    load(x_tok[rows, tau, :], t[0].rearrange("(c j) d -> j c d", j=CH)[j], "x_in")
            for j in range(CH):
                rows, tau = tok_rows(j, 1)
                load(h_tok[rows, tau, :], pos_d.rearrange("(c j) d -> j c d", j=CH)[j], "pos_in")
            sp.wait_ge(sem("cleared"), 4)
            sp.wait_ge(sem("cst_in"), 16)
            for s in range(2):
                for ch in range(6):
                    load(mod[s:P:32, ch * MODW:(ch + 1) * MODW],
                         b_ada[0, ch * D:(ch + 1) * D].rearrange("(q i) -> q i", q=4), "rows_in")
                for n, t in ((0, norm1_g), (1, norm2_g)):
                    load(gains[s:P:32, n, :], t[0].rearrange("(q i) -> q i", q=4), "rows_in")
            for g in range(4):
                lo = _C["wfbd"][0] + (g // 2) * P + (g % 2) * 64
                load(cst[64 * (g % 2):64 * (g % 2) + 64, lo:lo + 64], w_fnet[0, g], "wf_in")
            for n, (kind, j, b) in enumerate(early):
                u = n + 1
                if kind == "ada" and (j, b) == (2, 1):
                    sp.wait_ge(sem("kd_out"), 16)
                    sp.wait_ge(sem("scratch_dead"), 1)
                    load(wglu[:, :, :], w_glu[0].rearrange("(k p) c -> p k c", p=P), "wglu_in")
                if u >= 3:
                    sp.wait_ge(early_used[u % 3], u // 3)
                w = w_ada[0, :, j * D:(j + 1) * D] if kind == "ada" else w_in[0]
                sp.dma_start(ring[u % 3][:, :, :], w.rearrange("(b k p) c -> b p k c", b=2, p=P)[b])\
                  .then_inc(early_in[u % 3], 16)
            def first_expert(i):
                if i < 3:
                    last = max(n for n in early_id.values() if n % 3 == i)
                    sp.wait_ge(early_used[i], last // 3 + 1)
                sp.dma_start(ring[i][:, :, :], halves(W6[i][0], 0, W6[i][1])).then_inc(unit_in[i], 16)

            first_expert(0)
            sp.wait_ge(sem("s5_read"), 1)
            sp.wait_ge(sem("du_dead"), 6)
            load(wout[:, :, :], w_out[0].rearrange("(k p) c -> p k c", p=P), "wout_in")
            for i in range(3, 6):
                first_expert(i)
            load(wrt[:, :, :], w_router[0].rearrange("(k p) e -> p k e", p=P), "route_in")
            sp.wait_ge(sem("x2_ready"), 4)
            sp.wait_ge(sem("ss_ready"), 4)
            load(brt[:, :], b_router, "route_in")
            load(bdn[:, :], b_down[0], "route_in")
            for n in range(3):
                for i, t in ((0, b_gate), (1, b_up)):
                    load(braw[NE * n:NE * (n + 1), i, :], t[0], "braw_in")
            sp.wait_ge(sem("gain_dead"), 1)
            for s in range(2):
                load(gains[s:P:32, 0, :], norm_f_g.rearrange("(q i) -> q i", q=4), "gainf_in")
            first_expert(1)
            first_expert(2)
            sp.wait_ge(bank_full, first["o"] + 4)
            for i in range(2):
                sp.wait_ge(unit_in[i], 16)
                sp.dma_start(ring[6 + i][:, :, :], halves(W6[i][0], 1, W6[i][1])).then_inc(unit_in[i], 16)

            def refill(e, phase, i, done, done_before):
                sp.wait_ge(unit_in[i], 16 * e)
                if i >= 2:
                    sp.wait_ge(unit_used[i - 2], done)
                else:
                    sp.wait_ge(unit_used[i + 4], done_before)
                w = W6[i][0][0].rearrange("e (b k p) c -> e b p k c", b=2, p=P)
                sp.dma_start(ring[2 * pair_slot(phase, i // 2) + i % 2][:, :, :],
                             w[bass.ds(e, 1), W6[i][1]].rearrange("e p k c -> (e p) k c")).then_inc(unit_in[i], 16)

            def first_round(e):
                return sp.value_load(tbl[0:1, bass.ds(e + 2 * NRT, 1)], min_val=1, max_val=NR)

            sp.wait_ge(sem("tables"), 1)
            before = None
            for e in range(1, 4):
                done = first_round(e)
                for i in range(2 if e == 1 else 0, 6):
                    refill(e, e, i, done, before)
                before = done
            with sp.Fori(1, NE // 4) as quad:
                before = first_round(4 * quad - 1)
                for phase in range(4):
                    done = first_round(4 * quad + phase)
                    for i in range(6):
                        refill(4 * quad + phase, phase, i, done, before)
                    before = done
            sp.wait_ge(sem("y_ready"), 1)
            for j in (0, 1):
                store_tokens(sp, j)
            sp.wait_ge(sem("y_out"), 16 * 8)

        def scan(eng, chain, parts):
            count = [0]
            last = [0] * len(parts)

            def put(i, ins):
                count[0] += 1
                ins.then_inc(chain, 1)
                last[i] = count[0]

            def settle(i):
                if last[i]:
                    eng.wait_ge(chain, last[i])

            views = []
            for d, k0, k1 in parts:
                n = k1 - k0
                a = slice(d * NP + k0, d * NP + k1)
                views.append((scan_p[:, d, :, 2 * k0:2 * k1], scan_q[:, d, :, 2 * k0:2 * k1],
                              a4r[:, a].unsqueeze(2).broadcast_to([P, n, 2]).unsqueeze(1).broadcast_to([P, 2, n, 2]),
                              a4i[:, :, a].unsqueeze(3).broadcast_to([P, 2, n, 2])))
            v = lambda a: a.rearrange("p r (k s) -> p r k s", s=2)
            for step in range(NC):
                for stage in range(4):
                    for i, (d, k0, k1) in enumerate(parts):
                        tp, tq, ar, ai = views[i]
                        x = slice(2 * k0, 2 * k1)
                        prev, cur = (step, step + 1) if d == 0 else (NC - step, NC - 1 - step)
                        if stage == 0:
                            settle(i)
                            put(i, eng.tensor_tensor(v(tp), ar, v(SL[:, :, d, prev, x]), ALU.mult))
                        elif stage == 1:
                            put(i, eng.tensor_tensor(v(tq), ai, v(SL[:, ::-1, d, prev, x]), ALU.mult))
                        elif stage == 2:
                            settle(i)
                            put(i, eng.tensor_tensor(tp, tp, tq, ALU.add))
                        else:
                            settle(i)
                            put(i, eng.tensor_tensor(SL[:, :, d, cur, x], SL[:, :, d, cur, x], tp, ALU.add))
            for i in range(len(parts)):
                settle(i)

        def loc_out(copy, b, kb, r):
            for d in range(2):
                o = SL[:, r, d, 1 - d:1 - d + NC, 8 * kb:8 * kb + 8].rearrange("p c x -> p x c")
                ins = copy(o, b[:, d * 256:(d + 1) * 256].rearrange("p (x c) -> p x c", c=NC))
            return ins

        def twice(b):
            return b.rearrange("p (g h) -> p g h", h=HS).unsqueeze(2).broadcast_to([64, 24, 2, HS])

        def zc_view(i):
            return zc[:, :, P * i:P * (i + 1)].rearrange("p j (g h) -> p g j h", h=HS)

        @block.gpsimd
        def _(pool):
            n = [0]

            def link(ins):
                n[0] += 1
                ins.then_inc(sem("pool_chain"), 1)
                pool.wait_ge(sem("pool_chain"), n[0])

            pool.memset(mod[:, :], 0.0).then_inc(sem("cleared"), 1)
            pool.memset(gains[:, :, :], 0.0).then_inc(sem("cleared"), 1)
            pool.memset(bbx[0][:, :, :, :, :], 0.0).then_inc(sem("cleared"), 1)
            pool.memset(cs[:, :], 0.0).then_inc(sem("cleared"), 1)
            pool.wait_ge(sem("small_in"), 16 * 8)
            pool.tensor_copy(natT[:, :, :], rawT[:, :].unsqueeze(2).broadcast_to([G, 2, ST])).then_inc(sem("nat_rep"), 1)
            pool.tensor_copy(natD[:, :, :, :], rawD[:, :, :].unsqueeze(2).broadcast_to([NP, 2, CH, HS]))\
                .then_inc(sem("nat_rep"), 1)
            pool.wait_ge(sem("nat_rep"), 2)
            pool.wait_ge(sem("x_in"), 16 * 8)
            pool.wait_ge(sem("pos_in"), 16 * 4)
            for j in range(CH):
                rows, tau = tok_rows(j, 1)
                pool.tensor_tensor(x_tok[rows, tau, :], x_tok[rows, tau, :], h_tok[rows, tau, :], ALU.add)\
                    .then_inc(sem("pos_added"), 1)
                pool.wait_ge(sem("pos_added"), j + 1)
            pool.wait_ge(sem("powers"), 2)
            pool.wait_ge(sem("Ct_ready"), 4)
            for d in range(2):
                step = slice(None) if d == 0 else slice(None, None, -1)
                ar, ai = (Ap[:, r, step, d * NP:(d + 1) * NP].unsqueeze(2).broadcast_to([P, 5, HS, NP]) for r in range(2))
                cr, ci = (Ct[:, :, r * G + d * NP:r * G + (d + 1) * NP].unsqueeze(1).broadcast_to([P, 5, HS, NP])
                          for r in range(2))
                re, im = ca[:, d, 0], ca[:, d, 1]
                link(pool.tensor_tensor(re, cr, ar, ALU.mult))
                link(pool.tensor_tensor(tmpc[:, :, :, :], ci, ai, ALU.mult))
                link(pool.tensor_tensor(re, re, tmpc[:, :, :, :], ALU.subtract))
                link(pool.tensor_tensor(im, cr, ai, ALU.mult))
                link(pool.tensor_tensor(tmpc[:, :, :, :], ci, ar, ALU.mult))
                link(pool.tensor_tensor(tmpc[:, :, :, :], im, tmpc[:, :, :, :], ALU.add))
                link(pool.tensor_scalar(im, tmpc[:, :, :, :], -1.0, None, ALU.mult))
                pool.sem_inc(sem("ca_ready"), 1)
            pool.wait_ge(sem("windows"), 2)
            pool.dma_start(kd_dram.rearrange("(b r) c -> r b c", r=P), KK[:, :, :]).then_inc(sem("kd_out"), 16)
            pool.wait_ge(sem("kd_out"), 16)
            win = kd_dram.rearrange("(k g h) c -> g h k c", g=2, h=HS)
            for g2 in range(2):
                for j in range(CH):
                    r0 = 64 * g2 + 16 * j
                    pool.dma_start(T[r0:r0 + 16, :, :], win[g2, :, :, (3 - j) * HS:(7 - j) * HS])\
                        .then_inc(sem("T_in"), 16)
            pool.wait_ge(sem("U_ready"), 6)
            for g2 in range(2):
                rows = slice(64 * g2, 64 * g2 + 64)
                pool.tensor_tensor(DU[rows, :, :], U[rows, g2::2, :],
                                   dcol[rows, :].unsqueeze(2).broadcast_to([64, NP, TC]), ALU.mult)\
                    .then_inc(sem("du_ready"), 1)
                pool.wait_ge(sem("du_ready"), g2 + 1)
            pool.wait_ge(sem("loc_ready_act"), 6)
            pool.wait_ge(sem("loc_ready_dve"), 6)
            pool.wait_ge(sem("init_ready"), 1)
            scan(pool, sem("scan_pool_chain"), [(1, SPLIT, NP)])
            pool.sem_inc(sem("scan_pool"), 1)
            pool.wait_ge(sem("braw_in"), 16 * 6)
            pool.wait_ge(sem("y_filled"), 1)
            pool.wait_ge(sem("glu_filled"), 1)
            link(pool.tensor_copy(bias3[:, :, :], braw[:, :, :]))
            link(pool.tensor_tensor(r1[:, :, :], braw[:, :, :], bias3[:, :, :], ALU.subtract))
            pool.sem_inc(sem("bias_rest"), 1)
            pool.tensor_copy(bias3[32:64, :, :], r1[32:64, :, :]).then_inc(sem("bias_second"), 1)
            pool.wait_ge(sem("bias_third"), 1)
            link(pool.tensor_tensor(r1[64:96, :, :], r1[64:96, :, :], bias3[64:96, :, :], ALU.subtract))
            pool.tensor_copy(bias3[64:96, :, :], r1[64:96, :, :]).then_inc(sem("bias_last"), 1)
            pool.wait_ge(sem("bias_second"), 1)
            pool.wait_ge(sem("bias_last"), 1)
            pool.sem_inc(sem("bias_ready"), 1)


        @block.tensor
        def _(pe):
            ident = C("ident")

            def tr(out, src):
                k = src.shape[0]
                return pe.transpose(out, src, ident[0:k, 0:k])

            def full(ins):
                ins.then_inc(bank_full, 1)

            pe.wait_ge(sem("cst_in"), 16)
            pe.wait_ge(sem("small_in"), 16 * 8)
            pe.wait_ge(sem("nat_rep"), 2)
            b = claim(pe, "params")
            tr(b[:, 0:96], natL[:, :])
            tr(b[:, 96:192], natS[:, :])
            tr(b[:, 192:240], natT[:, :, :].rearrange("r g p -> r (g p)"))
            tr(b[:, 240:264], natD[:, :, :, :].rearrange("r g i h -> r (g i h)"))
            full(tr(b[:, 264:280], natCc[:, :]))
            pe.wait_ge(early_in[0], 32)
            for i in range(4):
                b = claim(pe, "B", i)
                for n in range(4):
                    ins = tr(b[:, n * 96:(n + 1) * 96], natB[:, :, 4 * i + n])
                full(ins)
            pe.wait_ge(sem("natC_in"), 64)
            for i in range(4):
                b = claim(pe, "Cc", i)
                for n in range(4):
                    ins = tr(b[:, n * 96:(n + 1) * 96], natC[:, 4 * i + n, :, :].rearrange("r g p -> r (g p)"))
                full(ins)
            pe.wait_ge(bank_full, first["Cc"] + 4)
            pe.sem_inc(early_used[0], 1)

            def mod_chunk(j):
                pe.wait_ge(sem("cs_ready"), 1)
                out = mod_bank(j)
                for b_ in range(2):
                    w = early_wait(pe, ("ada", j, b_))
                    for k in range(4):
                        kk = 4 * b_ + k
                        for q in range(4):
                            ins = pe.matmul(out[32 * q:32 * q + 32, :], cs[:, 2 * kk:2 * kk + 32],
                                            w[:, k, q * MODW:(q + 1) * MODW], start=(kk == 0), stop=(kk == 7),
                                            skip_group_check=True)
                    early_release(ins, ("ada", j, b_))
                pe.wait_ge(early_used[early_id[("ada", j, 1)] % 3], early_id[("ada", j, 1)] // 3 + 1)
                pe.sem_inc(sem("mod_filled"), 1)

            def gt_tables(d):
                pe.wait_ge(sem("gm_ready"), d + 1)
                g = gm[d][:, :, :, :, :].rearrange("p r j h k -> p (r j h) k")
                for i in range(6):
                    b = claim(pe, f"gt{d}", i)
                    for n in range(4):
                        ins = tr(b[:, n * P:(n + 1) * P], g[:, :, 4 * i + n])
                    full(ins)

            def spread(stage, rows):
                for q in range(4):
                    b = claim(pe, stage, q)
                    full(pe.matmul(b[:, 0:MODW], C("ssel", slice(32 * q, 32 * q + 32)), rows[32 * q:32 * q + 32, :],
                                   start=True, stop=True))

            mod_chunk(0)
            gt_tables(0)
            mod_chunk(1)
            gt_tables(1)
            pe.wait_ge(sem("wf_in"), 16 * 4)
            b = claim(pe, "m12")
            for t in range(2):
                wf = C("wfbd")[:, t * P:(t + 1) * P]
                pe.matmul(b[:, t * 256:t * 256 + P], C("ccbd"), wf, start=True, stop=True)
                ins = pe.matmul(b[:, t * 256 + P:(t + 1) * 256], C("nscbd"), wf, start=True, stop=True)
            full(ins)
            pe.wait_ge(sem("mod_rows"), 2)
            spread("gs1", mod[:, MODW:2 * MODW])
            spread("sh1", mod[:, 0:MODW])

            def turn_tokens(stage, src, ready):
                pe.wait_ge(sem(ready), 8)
                for i in range(4):
                    b = claim(pe, stage, i)
                    for k in range(2):
                        for tau in range(2):
                            ins = tr(b[:, k * 256 + tau * P:k * 256 + (tau + 1) * P],
                                     src[:, tau, (2 * i + k) * P:(2 * i + k + 1) * P])
                    full(ins)

            def kernels(d):
                pe.wait_ge(sem("bbx_ready"), d + 1)
                pe.wait_ge(sem("ca_ready"), d + 1)
                b = claim(pe, f"K{d}")
                m0 = 0 if d == 0 else 1
                for k in range(NP):
                    q, kb = k % 4, k // 4
                    for r in range(2):
                        ins = pe.matmul(b[32 * q:32 * q + 32, kb * 64:kb * 64 + 64],
                                        bbx[d][:, k, r, :, :].rearrange("p g h -> p (g h)"),
                                        ca[:, d, r, m0:m0 + 4, :, k].rearrange("p m h -> p (m h)"),
                                        start=(r == 0), stop=(r == 1))
                full(ins)

            kernels(0)
            turn_tokens("hT", h_tok, "h_ready")
            w0 = early_wait(pe, ("w_in", 0, 0))
            w1 = early_wait(pe, ("w_in", 0, 1))
            pe.wait_ge(sem("hT_ready"), 4)
            for tau in range(2):
                for n in range(2):
                    b = claim(pe, "u", 2 * tau + n)
                    for k in range(KD):
                        w = (w0, w1)[k // 4]
                        ins = pe.matmul(b[:, 0:384], hT[:, k, tau * P:(tau + 1) * P], w[:, k % 4, n * 384:(n + 1) * 384],
                                        start=(k == 0), stop=(k == KD - 1))
                    full(ins)
            kernels(1)
            pe.wait_ge(sem("uc_ready_dve"), 4)
            pe.wait_ge(sem("uc_ready_act"), 4)
            for i in range(6):
                b = claim(pe, "U", i)
                for n in range(8):
                    ins = tr(b[:, n * 64:(n + 1) * 64], uc[:, 8 * i + n, :, :, :].rearrange("p r j h -> p (r j h)"))
                full(ins)
            pe.wait_ge(sem("U_ready"), 6)
            pe.wait_ge(sem("GT_ready"), 12)
            for kb in range(6):
                for r in range(2):
                    b = claim(pe, "loc", 2 * kb + r)
                for d in range(2):
                    for q in range(4):
                        k = 4 * kb + q
                        for g2 in range(2):
                            for r in range(2):
                                rows = slice(64 * r, 64 * r + 64)
                                last_r = pe.matmul(
                                    bank("loc", 2 * kb + r)[64 * g2:64 * g2 + 64, (4 * d + q) * 64:(4 * d + q + 1) * 64],
                                    GT[rows, d * NP + k, 64 * g2:64 * g2 + 64], U[rows, 2 * k + g2, :],
                                    start=True, stop=True)
                                if d == 1 and q == 3 and g2 == 1:
                                    full(last_r)
            b = claim(pe, "uf")
            for t in range(2):
                for k in range(KD):
                    w = (w0, w1)[k // 4]
                    ins = pe.matmul(b[:, t * 256:(t + 1) * 256], w[:, k % 4, DS5 + t * P:DS5 + (t + 1) * P], hT[:, k, :],
                                    start=(k == 0), stop=(k == KD - 1))
            full(ins)
            pe.wait_ge(bank_full, first["uf"] + 1)
            pe.sem_inc(early_used[early_id[("w_in", 0, 0)] % 3], 1)
            pe.sem_inc(early_used[early_id[("w_in", 0, 1)] % 3], 1)
            pe.wait_ge(sem("ufT_ready"), 1)
            pe.wait_ge(sem("m12_ready"), 1)
            m12 = cst[:, _C["ccbd"][0]:_C["ccbd"][0] + 512]
            for s in range(2):
                b = claim(pe, "Z", s)
                for t in range(2):
                    ins = pe.matmul(b[:, t * 256:(t + 1) * 256], ufT[:, t, s, :], m12[:, t * 256:(t + 1) * 256], start=True, stop=True)
                full(ins)
            pe.wait_ge(sem("Zs_ready"), 2)
            b = claim(pe, "yf")
            for t in range(2):
                for s in range(2):
                    o = b[:, t * 256:(t + 1) * 256].rearrange("p (j s c) -> p s j c", s=2, c=NC)[:, s]
                    pe.matmul(o, Zs[:, s, t, 0:P], C("cosL"), start=True, stop=False)
                    ins = pe.matmul(o, Zs[:, s, t, P:2 * P], C("sinL"), start=False, stop=True)
            full(ins)
            for j in range(2, 5):
                mod_chunk(j)
            def y_part(kb):
                for g2 in range(2):
                    claim(pe, f"y{kb}", g2)
                for kk in range(8):
                    k = 8 * kb + kk
                    for n in range(5):
                        for g2 in range(2):
                            rows = slice(64 * g2, 64 * g2 + 64)
                            o = bank(f"y{kb}", g2)[rows, kk * 64:(kk + 1) * 64]
                            if n == 0:
                                pe.matmul(o, T[rows, k, :], U[rows, 2 * k + g2, :], start=True, stop=False)
                                continue
                            d, r = (n - 1) // 2, (n - 1) % 2
                            m0 = 1 if d == 0 else 0
                            lhs = ca[rows, d, r, m0:m0 + 4, :, k].rearrange("p m h -> p (m h)")
                            st = SL[rows, r, d, d:d + NC, 2 * k:2 * k + 2].rearrange("p c s -> p s c")
                            ins = pe.matmul(o, lhs, st, start=False, stop=(n == 4))
                            if n == 4 and kk == 7:
                                full(ins)

            pe.wait_ge(sem("T_in"), 16 * 8)
            pe.wait_ge(sem("scan_dve"), 1)
            pe.wait_ge(sem("scan_pool"), 1)
            y_part(0)
            y_part(1)
            pe.wait_ge(sem("fs_ready"), 1)
            b = claim(pe, "fin")
            full(tr(b[0:96, 0:P], fs[:, :, :].rearrange("p r k -> p (r k)")))
            y_part(2)
            pe.wait_ge(bank_full, first["y2"] + 2)
            pe.sem_inc(sem("s5_read"), 1)
            pe.sem_inc(sem("y_filled"), 1)
            for i in range(6):
                pe.wait_ge(sem("z_ready"), 2 * (i // 2) + 2)
                b = claim(pe, "zc", i)
                for n in range(4):
                    ins = tr(b[0:64, n * P:(n + 1) * P], Zg[:, 4 * i + n, :])
                full(ins)
            pe.wait_ge(sem("zc_ready"), 6)
            for i in range(3):
                b = claim(pe, "zT", i)
                for t in range(2):
                    for j in range(CH):
                        ct = 2 * i + t
                        ins = tr(b[:, t * 256 + j * 64:t * 256 + (j + 1) * 64], zc[:, j, ct * P:(ct + 1) * P])
                full(ins)
            pe.wait_ge(sem("wglu_in"), 16)
            pe.wait_ge(sem("zT_ready"), 3)
            for i in range(3):
                b = claim(pe, "glu", i)
                for t in range(2):
                    ct = 2 * i + t
                    for k in range(NCT):
                        ins = pe.matmul(b[:, t * 256:(t + 1) * 256], wglu[:, k, ct * P:(ct + 1) * P], zT[:, k, :],
                                        start=(k == 0), stop=(k == NCT - 1))
                full(ins)
            pe.wait_ge(bank_full, first["glu"] + 3)
            pe.sem_inc(sem("glu_filled"), 1)
            pe.wait_ge(sem("mod_rows"), 5)
            spread("g1", mod[:, 2 * MODW:3 * MODW])
            pe.wait_ge(sem("wout_in"), 16)
            pe.wait_ge(sem("yc_ready"), 3)
            pe.wait_ge(sem("yf_ready"), 1)
            for tau in range(2):
                for dh in range(2):
                    b = claim(pe, "o", 2 * tau + dh)
                    for k in range(KD):
                        ins = pe.matmul(b, ycT[:, k, tau * P:(tau + 1) * P], wout[:, k, dh * HALF:(dh + 1) * HALF],
                                        start=(k == 0), stop=(k == KD - 1))
                    full(ins)
            spread("gs2", mod[:, 4 * MODW:5 * MODW])
            spread("sh2", mod[:, 3 * MODW:4 * MODW])
            mod_chunk(5)
            turn_tokens("h2T", h2, "h2_ready")
            pe.wait_ge(sem("route_in"), 16 * 3)
            pe.wait_ge(sem("h2T_ready"), 4)
            b = claim(pe, "lg")
            for tau in range(2):
                o = b[:, tau * NE:(tau + 1) * NE]
                pe.matmul(o, C("ones", slice(0, 1)), brt[:, :], start=True, stop=False)
                for k in range(KD):
                    ins = pe.matmul(o, hT[:, k, tau * P:(tau + 1) * P], wrt[:, k, :], start=False, stop=(k == KD - 1))
            full(ins)
            pe.wait_ge(sem("gainf_in"), 32)
            pe.wait_ge(sem("mod_rows"), 6)
            for q in range(4):
                rows = slice(32 * q, 32 * q + 32)
                b = claim(pe, "end", q)
                pe.matmul(b[:, 0:MODW], C("ssel", rows), mod[rows, 5 * MODW:6 * MODW], start=True, stop=True)
                full(pe.matmul(b[:, MODW:2 * MODW], C("ssel", rows), gains[rows, 0, :], start=True, stop=True))
            pe.wait_ge(sem("mask_ready"), 1)
            b = claim(pe, "rk")
            pe.matmul(b[:, 0:NE], C("triu"), gt[:, 0, :], start=True, stop=True)
            pe.matmul(b[:, NE:2 * NE], C("ones"), gt[:, 0, :], start=True, stop=False)
            pe.matmul(b[:, NE:2 * NE], C("triu"), gt[:, 1, :], start=False, stop=True)
            for tau in range(2):
                ins = pe.matmul(b[0:NE, 64:65], gt[:, tau, :], C("ones")[:, 0:1], start=(tau == 0), stop=(tau == 1))
            full(ins)
            pe.wait_ge(sem("rounds_ready"), 1)
            b = claim(pe, "cu")
            full(pe.matmul(b[0:NE, 0:1], C("triu", slice(0, NE))[:, 0:NE], cnt[:, 1:2], start=True, stop=True))
            pe.wait_ge(sem("cmp_ready"), 1)
            b = claim(pe, "tb")
            pe.matmul(b[0:1, 0:NRT], C("ones", slice(0, NE))[:, 0:1], cmp[:, 0:NRT], start=True, stop=True)
            pe.matmul(b[0:1, NRT:2 * NRT], cnt[:, 1:2], cmp[:, 0:NRT], start=True, stop=True)
            pe.matmul(b[0:1, 2 * NRT + NE:2 * NRT + NE + 1], cnt[:, 1:2], C("ones", slice(0, NE))[:, 0:1], start=True, stop=True)
            full(pe.matmul(b[0:1, 2 * NRT:2 * NRT + NE], cnt[:, 1:2], C("triu", slice(0, NE))[:, 0:NE],
                           start=True, stop=True))
            pe.wait_ge(sem("comb_ready"), 1)
            b = claim(pe, "cb")
            for tau in range(2):
                ins = tr(b[0:NE, tau * P:(tau + 1) * P], comb[:, tau, :])
            full(ins)
            pe.wait_ge(sem("tables"), 1)
            total = pe.value_load(tbl[0:1, 2 * NRT + NE:2 * NRT + NE + 1], min_val=NE, max_val=NR)

            def gather(r):
                pe.wait_ge(sem("sel_ready"), r + 1)
                for tau in range(2):
                    for dh in range(2):
                        ins = pe.matmul(pX[64 * dh:64 * dh + 64, :], sel[:, tau, :],
                                        h2[:, tau, dh * HALF:(dh + 1) * HALF], start=(tau == 0), stop=(tau == 1),
                                        skip_group_check=True)
                ins.then_inc(sem("gathered"), 1)

            def turn_x(r):
                pe.wait_ge(sem("Xs_ready"), r + 1)
                for n in range(4):
                    ins = tr(pT[:, n * P:(n + 1) * P], Xs[:, n * P:(n + 1) * P])
                ins.then_inc(sem("X_turned"), 1)

            def scatter(r):
                pe.wait_ge(sem("ys_ready"), r + 2)
                pe.wait_ge(sem("selT_ready"), r + 2)
                for tau in range(2):
                    for dh in range(2):
                        rows = slice(64 * dh, 64 * dh + 64)
                        ins = pe.matmul(OUT[tau][dh], selT[rows, tau * P:(tau + 1) * P], ys[rows, :],
                                        start=False, stop=False, skip_group_check=True)
                ins.then_inc(sem("scattered"), 1)

            def expert_round(R, e, phase):
                def w(i):
                    return ring[2 * pair_slot(phase, i // 2) + i % 2]

                pe.wait_ge(sem("XT_ready"), R + 1)
                pe.wait_ge(sem("selb_ready"), R + 1)
                for m, out in ((0, pG), (1, pU)):
                    if m == 1:
                        pe.wait_ge(sem("selT_ready"), R + 1)
                    for fh in range(2):
                        pe.matmul(out[64 * fh:64 * fh + 64, :], selb[:, :], bias3[:, m, fh * HALF:(fh + 1) * HALF],
                                  start=True, stop=False, skip_group_check=True)
                    for k in range(KD):
                        i = 2 * m + k // 4
                        if k % 4 == 0:
                            pe.wait_ge(unit_in[i], 16 * e + 16)
                        for fh in range(2):
                            ins = pe.matmul(out[64 * fh:64 * fh + 64, :], XT[:, k % 4, (k // 4) * 64:(k // 4) * 64 + 64],
                                            w(i)[:, k % 4, fh * HALF:(fh + 1) * HALF], start=False,
                                            stop=(k == KD - 1), skip_group_check=True)
                        if k % 4 == 3:
                            ins.then_inc(unit_used[i], 1)
                    if m == 0:
                        pe.wait_ge(sem("ys_ready"), R + 1)
                        gather(R + 1)
                scatter(R - 1)
                pe.wait_ge(sem("act_ready"), R + 1)
                for n in range(4):
                    ins = tr(pG[:, n * P:(n + 1) * P], acts[:, n * P:(n + 1) * P])
                ins.then_inc(sem("act_turned"), 1)
                turn_x(R + 1)
                pe.wait_ge(sem("selw_ready"), R + 1)
                for tau in range(2):
                    ins = tr(pU[:, tau * P:(tau + 1) * P], selw[:, tau, :, :].rearrange("p a b -> p (a b)"))
                ins.then_inc(sem("sel_turned"), 1)
                pe.wait_ge(sem("actT_ready"), R + 1)
                for k in range(KD):
                    i = 4 + k // 4
                    if k % 4 == 0:
                        pe.wait_ge(unit_in[i], 16 * e + 16)
                    for dh in range(2):
                        ins = pe.matmul(pX[64 * dh:64 * dh + 64, :], actT[:, k % 4, (k // 4) * 64:(k // 4) * 64 + 64],
                                        w(i)[:, k % 4, dh * HALF:(dh + 1) * HALF], start=(k == 0), stop=(k == KD - 1),
                                        skip_group_check=True)
                    if k % 4 == 3:
                        ins.then_inc(unit_used[i], 1)

            gather(0)
            pe.wait_ge(sem("combT_ready"), 1)
            for bb in range(NB):
                pe.wait_ge(bank_drained[bb], len([n for n in range(njobs) if n % NB == bb]))
            for tau in range(2):
                for dh in range(2):
                    ins = pe.matmul(OUT[tau][dh], combT[:, tau * P:(tau + 1) * P], bdn[:, dh * HALF:(dh + 1) * HALF],
                                    start=True, stop=False, skip_group_check=True)
            ins.then_inc(sem("combT_used"), 1)
            turn_x(0)
            pe.wait_ge(sem("bias_ready"), 1)

            def round_start(e):
                return pe.value_load(tbl[0:1, bass.ds(e + 2 * NRT, 1)], min_val=0, max_val=NR)

            with pe.Fori(0, NE // 4) as quad:
                for phase in range(4):
                    e = 4 * quad + phase
                    with pe.Fori(round_start(e), round_start(e + 1)) as R:
                        expert_round(R, e, phase)
            scatter(total - 1)

        @block.scalar
        def _(act):
            act.wait_ge(sem("PT_ready"), 1)
            act.activation(sc[:, 1, :], PT[:, 192:240], ACT.Exp).then_inc(sem("dt_ready"), 1)
            act.wait_ge(sem("er_ready"), 1)
            act.activation(sc[:, 4, :], sc[:, 3, :], ACT.Exp).then_inc(sem("mag_ready"), 1)
            act.activation(cT[:, :], PT[:, 264:280], ACT.Sigmoid).then_inc(sem("sig_ready"), 1)
            act.wait_ge(sem("angle_ready"), 1)
            act.activation(sc[:, 8:10, :], sc[:, 6:8, :], ACT.Sin).then_inc(sem("sin_ready"), 1)
            for i in range(4):
                b = filled(act, "Cc", i)
                ins = act.copy(Ct[:, 4 * i:4 * i + 4, :], b[:, 0:384].rearrange("p (h x) -> p h x", x=96))
                drained(ins, "Cc", i)
            act.wait_ge(bank_drained[(first["Cc"] + 3) % NB], (first["Cc"] + 3) // NB + 1)
            act.sem_inc(sem("Ct_ready"), 4)
            act.wait_ge(sem("pos_added"), 4)
            for tau in range(2):
                act.activation(h_tok[:, tau, :], x_tok[:, tau, :], ACT.Square, accum_out=ss[:, tau:tau + 1])\
                    .then_inc(sem("ss_ready"), 1)
            for d in range(2):
                if d == 1:
                    act.wait_ge(sem("ms_ready"), 1)
                    act.activation(ss[:, 4:6], ss[:, 2:4], ACT.Sqrt).then_inc(sem("rms_ready"), 1)
                for i in range(6):
                    b = filled(act, f"gt{d}", i)
                    k = d * NP + 4 * i
                    drained(act.copy(GT[:, k:k + 4, :], b.rearrange("p (k x) -> p k x", x=P)), f"gt{d}", i)
            act.wait_ge(bank_drained[(first["gt1"] + 5) % NB], (first["gt1"] + 5) // NB + 1)
            act.sem_inc(sem("GT_ready"), 12)
            for i in (1, 3):
                b = filled(act, "hT", i)
                ins = act.copy(hT[:, 2 * i:2 * i + 2, :], b.rearrange("p (k x) -> p k x", x=256))
                drained(ins, "hT", i)
                act.wait_ge(bank_drained[(first["hT"] + i) % NB], (first["hT"] + i) // NB + 1)
                act.sem_inc(sem("hT_ready"), 1)

            def copy_signal(dst, src, stage, i, s):
                drained(act.copy(dst, src), stage, i)
                n = first[stage] + i
                act.wait_ge(bank_drained[n % NB], n // NB + 1)
                act.sem_inc(sem(s), 1)

            act.wait_ge(sem("uc_free"), 1)
            for i in range(4):
                b = filled(act, "u", i)
                tau, n = i // 2, i % 2
                act.copy(uc[:, 24 * n:24 * n + 24, :, 2 * tau + 1, :], twice(b[64:128, 0:384]))\
                    .then_inc(sem("uc_ready_act"), 1)
            for i in (1, 3, 5):
                b = filled(act, "U", i)
                copy_signal(U[:, 8 * i:8 * i + 8, :], b.rearrange("p (g x) -> p g x", x=TC), "U", i, "U_ready")
            act.wait_ge(sem("U_ready"), 6)
            for kb in range(6):
                b = filled(act, "loc", 2 * kb + 1)
                n = first["loc"] + 2 * kb + 1
                drained(loc_out(act.copy, b, kb, 1), "loc", 2 * kb + 1)
                act.wait_ge(bank_drained[n % NB], n // NB + 1)
                act.sem_inc(sem("loc_ready_act"), 1)
            b = filled(act, "uf")
            for t in range(2):
                ins = act.copy(ufT[:, t, :, :].rearrange("p s (j c) -> p s j c", c=NC),
                               b[:, t * 256:(t + 1) * 256].rearrange("p (j s c) -> p s j c", s=2, c=NC))
            drained(ins, "uf")
            act.wait_ge(bank_drained[first["uf"] % NB], first["uf"] // NB + 1)
            act.sem_inc(sem("ufT_ready"), 1)
            for s in range(2):
                b = filled(act, "Z", s)
                copy_signal(Zs[:, s, :, :], b.rearrange("p (t x) -> p t x", x=256), "Z", s, "Zs_ready")
            b = filled(act, "yf")
            copy_signal(ycT[:, NCT:KD, :], b.rearrange("p (t x) -> p t x", x=256), "yf", 0, "yf_ready")
            for kb in range(3):
                if kb == 2:
                    b = filled(act, "fin")
                    copy_signal(fso[:, :], b[0:96, 0:P], "fin", 0, "fso_ready")
                    act.wait_ge(sem("fso_ready"), 1)
                    for half, t in ((0, new_re), (1, new_im)):
                        act.dma_start(t.rearrange("a b d (k g) p -> (a b d k) (g p)", g=2), fso[half * G:(half + 1) * G, :])\
                            .then_inc(sem("state_out"), 16)
                act.wait_ge(sem("yb_ready"), 2 * kb + 2)
                act.activation(Zg[:, 8 * kb:8 * kb + 8, :], DU[:, 8 * kb:8 * kb + 8, :], ACT.Gelu_apprx_tanh)\
                    .then_inc(sem("z_ready"), 2)
            act.wait_ge(sem("z_ready"), 6)
            act.sem_inc(sem("du_dead"), 6)
            for i in (1, 3, 5):
                b = filled(act, "zc", i)
                copy_signal(zc_view(i), b[0:64, :].rearrange("p (g j h) -> p g j h", j=CH, h=HS), "zc", i, "zc_ready")
            act.wait_ge(sem("state_out"), 32)
            b = filled(act, "zT", 1)
            copy_signal(zT[:, 2:4, :], b.rearrange("p (t x) -> p t x", x=256), "zT", 1, "zT_ready")
            for i in range(3):
                b = filled(act, "glu", i)
                drained(act.activation(ycT[:, 2 * i:2 * i + 2, :], b.rearrange("p (t x) -> p t x", x=256), ACT.Sigmoid),
                        "glu", i)
                n = first["glu"] + i
                act.wait_ge(bank_drained[n % NB], n // NB + 1)
                act.sem_inc(sem("sg_ready"), 1)
            for q in range(4):
                b = filled(act, "g1", q)
                copy_signal(g1s[:, q * MODW:(q + 1) * MODW], b[:, 0:MODW], "g1", q, "g1_ready")
            for tau in range(2):
                act.wait_ge(sem("x2_ready"), 2 * tau + 2)
                act.activation(sqj[:, :], x_tok[:, tau, :], ACT.Square, accum_out=ss[:, tau:tau + 1])\
                    .then_inc(sem("ss_ready"), 1)
                act.wait_ge(sem("ss_ready"), 3 + tau)
            act.wait_ge(sem("ms_ready"), 2)
            act.activation(ss[:, 4:6], ss[:, 2:4], ACT.Sqrt).then_inc(sem("rms_ready"), 1)
            for i in (1, 3):
                b = filled(act, "h2T", i)
                copy_signal(hT[:, 2 * i:2 * i + 2, :], b.rearrange("p (k x) -> p k x", x=256), "h2T", i, "h2T_ready")
            act.wait_ge(sem("lmax_ready"), 1)
            act.activation(ex[:, :, :], eq[0][:, :, :], ACT.Exp).then_inc(sem("ex_ready"), 1)
            for q in range(4):
                b = filled(act, "end", q)
                act.copy(g2s[:, q * MODW:(q + 1) * MODW], b[:, 0:MODW]).then_inc(sem("g2_ready"), 1)
                copy_signal(gfs[:, q * MODW:(q + 1) * MODW], b[:, MODW:2 * MODW], "end", q, "gainf_ready")
            act.wait_ge(sem("bias_rest"), 1)
            act.copy(bias3[64:96, :, :], r1[64:96, :, :]).then_inc(sem("bias_third"), 1)
            act.wait_ge(sem("tables"), 1)
            total = act.value_load(tbl[0:1, 2 * NRT + NE:2 * NRT + NE + 1], min_val=NE, max_val=NR)

            def empty_x(r):
                act.wait_ge(sem("gathered"), r + 1)
                act.copy(Xs[:, :], pX).then_inc(sem("Xs_ready"), 1)

            empty_x(0)
            with act.Fori(0, total) as R:
                act.wait_ge(sem("gcl_ready"), R + 1)
                act.activation(sgm[:, :], gcl[:, :], ACT.Sigmoid, scale=1.702).then_inc(sem("sgm_ready"), 1)
                empty_x(R + 1)
                act.wait_ge(sem("sel_turned"), R + 1)
                act.copy(selT[:, :], pU[:, 0:2 * P]).then_inc(sem("selT_ready"), 1)
                act.wait_ge(unit_used[5], R + 1)
                act.copy(ys[:, :], pX).then_inc(sem("ys_ready"), 1)
            for tau in range(2):
                act.wait_ge(sem("x3_ready"), 2 * tau + 2)
                act.activation(sqj[:, :], x_tok[:, tau, :], ACT.Square, accum_out=ss[:, tau:tau + 1])\
                    .then_inc(sem("ss_ready"), 1)
                act.wait_ge(sem("ss_ready"), 5 + tau)
            act.wait_ge(sem("ms_ready"), 3)
            act.activation(ss[:, 4:6], ss[:, 2:4], ACT.Sqrt).then_inc(sem("rms_ready"), 1)
            act.wait_ge(sem("y_ready"), 2)
            for j in (2, 3):
                store_tokens(act, j)
            act.wait_ge(sem("y_out"), 16 * 8)
            act.wait_ge(sem("state_out"), 32)

        @block.vector
        def _(dve):
            n_ = [0]

            def link(ins):
                n_[0] += 1
                ins.then_inc(sem("dve_chain"), 1)
                dve.wait_ge(sem("dve_chain"), n_[0])

            def tt(o, a, b_, op):
                link(dve.tensor_tensor(o, a, b_, op))

            def copy_signal(dst, src, stage, i, s):
                drained(dve.tensor_copy(dst, src), stage, i)
                n = first[stage] + i
                dve.wait_ge(bank_drained[n % NB], n // NB + 1)
                dve.sem_inc(sem(s), 1)

            v = lambda i: sc[:, i, :]
            b = filled(dve, "params")
            copy_signal(PT[:, 0:280], b[:, 0:280], "params", 0, "PT_ready")
            lr, li = PT[:, 0:48], PT[:, 48:96]
            link(dve.tensor_scalar(v(0), lr, -1e-4, None, ALU.min))
            dve.wait_ge(sem("dt_ready"), 1)
            tt(v(3), v(0), v(1), ALU.mult)
            dve.sem_inc(sem("er_ready"), 1)
            tt(v(2), li, v(1), ALU.mult)
            link(dve.tensor_scalar(v(5), v(2), 1.0 / TWO_PI, ROUND_MAGIC, ALU.mult, ALU.add))
            link(dve.tensor_scalar(v(5), v(5), -ROUND_MAGIC, None, ALU.add))
            link(dve.scalar_tensor_tensor(out=v(6), in0=v(5), scalar=-C1, in1=v(2), op0=ALU.mult, op1=ALU.add))
            link(dve.scalar_tensor_tensor(out=v(6), in0=v(5), scalar=-C2, in1=v(6), op0=ALU.mult, op1=ALU.add))
            link(dve.scalar_tensor_tensor(out=v(6), in0=v(5), scalar=-C3, in1=v(6), op0=ALU.mult, op1=ALU.add))
            link(dve.tensor_scalar(v(6), v(6), 3.1415925, -3.1415925, ALU.min, ALU.max))
            link(dve.tensor_scalar(v(7), v(6), -1.0, None, ALU.mult))
            tt(v(7), v(7), v(6), ALU.max)
            link(dve.tensor_scalar(v(7), v(7), -1.0, math.pi / 2, ALU.mult, ALU.add))
            dve.sem_inc(sem("angle_ready"), 1)
            tt(v(10), v(0), v(0), ALU.mult)
            tt(v(11), li, li, ALU.mult)
            tt(v(10), v(10), v(11), ALU.add)
            link(dve.reciprocal(v(10), v(10)))
            dve.wait_ge(sem("sig_ready"), 1)
            tt(cs[:, 0:16].rearrange("p (k s) -> p s k", s=2), PT[:, 264:280].rearrange("p (s k) -> p s k", s=2),
               cT[:, :].rearrange("p (s k) -> p s k", s=2), ALU.mult)
            dve.sem_inc(sem("cs_ready"), 1)
            link(dve.memset(Ap[:, 0, 0, :], 1.0))
            link(dve.memset(Ap[:, 1, 0, :], 0.0))
            dve.wait_ge(sem("mag_ready"), 1)
            dve.wait_ge(sem("sin_ready"), 1)
            A = lambda r, m: Ap[:, r, m, :]
            tt(A(0, 1), v(4), v(9), ALU.mult)
            tt(A(1, 1), v(4), v(8), ALU.mult)

            def cmul(ore, oim, ar, ai, br, bi, t):
                tt(ore, ar, br, ALU.mult)
                tt(t, ai, bi, ALU.mult)
                tt(ore, ore, t, ALU.subtract)
                tt(oim, ar, bi, ALU.mult)
                tt(t, ai, br, ALU.mult)
                tt(oim, oim, t, ALU.add)

            cmul(A(0, 2), A(1, 2), A(0, 1), A(1, 1), A(0, 1), A(1, 1), v(5))
            cmul(A(0, 3), A(1, 3), A(0, 2), A(1, 2), A(0, 1), A(1, 1), v(5))
            cmul(A(0, 4), A(1, 4), A(0, 2), A(1, 2), A(0, 2), A(1, 2), v(5))
            dve.sem_inc(sem("powers"), 2)
            link(dve.tensor_scalar(v(12), A(0, 1), -1.0, None, ALU.add))
            tt(v(13), v(12), v(0), ALU.mult)
            tt(v(5), A(1, 1), li, ALU.mult)
            tt(v(13), v(13), v(5), ALU.add)
            tt(v(13), v(13), v(10), ALU.mult)
            tt(v(14), A(1, 1), v(0), ALU.mult)
            tt(v(5), v(12), li, ALU.mult)
            tt(v(14), v(14), v(5), ALU.subtract)
            tt(v(14), v(14), v(10), ALU.mult)
            bc = lambda a: a.unsqueeze(1).broadcast_to([P, CH, G])
            cmul(Fp[:, 0], Fp[:, 1], bc(v(13)), bc(v(14)), Ap[:, 0, 0:CH, :], Ap[:, 1, 0:CH, :], sc[:, 5:9, :])
            link(dve.tensor_copy(a4r[:, :], A(0, 4)))
            link(dve.tensor_copy(a4i[:, 1, :], A(1, 4)))
            link(dve.tensor_scalar(a4i[:, 0, :], A(1, 4), -1.0, None, ALU.mult))
            link(dve.tensor_copy(dcol[:, :], PT[:, 240:264]))
            for i in range(4):
                b = filled(dve, "B", i)
                ins = dve.tensor_copy(Bt[:, 4 * i:4 * i + 4, :], b[:, 0:384].rearrange("p (h x) -> p h x", x=96))
                drained(ins, "B", i)
            n = first["B"] + 3
            dve.wait_ge(bank_drained[n % NB], n // NB + 1)

            def bbx_fill(d):
                j0 = CH - 1 if d == 0 else 0
                if d == 0:
                    dve.wait_ge(sem("cleared"), 4)
                else:
                    dve.wait_ge(bank_full, first["gt0"] + 6)
                    link(dve.memset(bbx[1][:, :, :, :, :], 0.0))
                for g2 in range(2):
                    rows = slice(64 * g2, 64 * g2 + 64)
                    for r in range(2):
                        link(dve.tensor_copy(bbx[d][rows, :, r, g2, :].rearrange("p k h -> p h k"), gm[d][rows, r, j0, :, :]))
                dve.sem_inc(sem("bbx_ready"), 1)

            for d in range(2):
                step = slice(None, None, -1) if d == 0 else slice(None)
                wr, wi = (Fp[:, r, step, d * NP:(d + 1) * NP].unsqueeze(2).broadcast_to([P, CH, HS, NP]) for r in range(2))
                br, bi = (Bt[:, :, r * G + d * NP:r * G + (d + 1) * NP].unsqueeze(1).broadcast_to([P, CH, HS, NP])
                          for r in range(2))
                cmul(gm[d][:, 0], gm[d][:, 1], wr, wi, br, bi, tmpg[:, :, :, :])
                dve.sem_inc(sem("gm_ready"), 1)
                bbx_fill(d)

            def norm_scale(nth):
                dve.wait_ge(sem("ss_ready"), 2 * nth)
                link(dve.tensor_scalar(ss[:, 2:4], ss[:, 0:2], 1.0 / D, EPS, ALU.mult, ALU.add))
                dve.sem_inc(sem("ms_ready"), 1)
                dve.wait_ge(sem("rms_ready"), nth)
                link(dve.reciprocal(ss[:, 6:8], ss[:, 4:6]))

            def mod_rows(j, gain=None):
                dve.wait_ge(sem("mod_filled"), (2, 2, 4, 4, 5, 6)[j])
                m = mod[:, j * MODW:(j + 1) * MODW]
                tt(m, mod_bank(j), m, ALU.add)
                if gain is not None:
                    link(dve.scalar_tensor_tensor(out=m, in0=m, scalar=1.0, in1=gains[:, gain, :], op0=ALU.add, op1=ALU.mult))
                dve.sem_inc(sem("mod_rows"), 1)

            def modulate(dst, s_gs, s_sh, ready):
                for q in range(4):
                    b = filled(dve, s_gs, q)
                    for tau in range(2):
                        ins = dve.scalar_tensor_tensor(out=dst[:, tau, q * MODW:(q + 1) * MODW],
                                                       in0=x_tok[:, tau, q * MODW:(q + 1) * MODW],
                                                       scalar=ss[:, 6 + tau:7 + tau], in1=b[:, 0:MODW],
                                                       op0=ALU.mult, op1=ALU.mult)
                    drained(ins, s_gs, q)
                n = first[s_gs] + 3
                dve.wait_ge(bank_drained[n % NB], n // NB + 1)
                for q in range(4):
                    b = filled(dve, s_sh, q)
                    for tau in range(2):
                        h = dst[:, tau, q * MODW:(q + 1) * MODW]
                        link(dve.tensor_tensor(h, h, b[:, 0:MODW], ALU.add))
                        dve.sem_inc(sem(ready), 1)
                    dve.sem_inc(bank_drained[(first[s_sh] + q) % NB], 1)

            norm_scale(1)
            dve.wait_ge(sem("rows_in"), 16 * 16)
            mod_rows(0)
            mod_rows(1, 0)
            dve.sem_inc(sem("gain_dead"), 1)
            b = filled(dve, "m12")
            copy_signal(cst[:, _C["ccbd"][0]:_C["ccbd"][0] + 512], b, "m12", 0, "m12_ready")
            modulate(h_tok, "gs1", "sh1", "h_ready")
            b = filled(dve, "K0").rearrange("p (b x) -> p b x", x=64)[:, 0:6, :]
            drained(dve.tensor_copy(KK[:, :, 48:112], b), "K0")
            n = first["K0"]
            dve.wait_ge(bank_drained[n % NB], n // NB + 1)
            dve.sem_inc(sem("windows"), 1)
            for i in (0, 2):
                b = filled(dve, "hT", i)
                copy_signal(hT[:, 2 * i:2 * i + 2, :], b.rearrange("p (k x) -> p k x", x=256), "hT", i, "hT_ready")
            dve.wait_ge(bank_full, first["hT"] + 4)
            link(dve.tensor_copy(ist[:, :, :], PT[:, 96:192].rearrange("p (r k) -> p r k", r=2)))
            dve.wait_ge(sem("ca_ready"), 2)
            dve.sem_inc(sem("uc_free"), 1)
            dve.sem_inc(sem("scratch_dead"), 1)
            for i in range(4):
                b = filled(dve, "u", i)
                tau, n = i // 2, i % 2
                link(dve.tensor_copy(uc[:, 24 * n:24 * n + 24, :, 2 * tau, :], twice(b[0:64, 0:384])))
                dve.sem_inc(sem("uc_ready_dve"), 1)
                dve.wait_ge(sem("uc_ready_act"), i + 1)
                dve.sem_inc(bank_drained[(first["u"] + i) % NB], 1)
            b = filled(dve, "K1").rearrange("p (b x) -> p b x", x=64)[:, 0:6, :]
            dve.tensor_copy(KK[:, :, 0:48], b[:, :, 0:48])
            drained(dve.tensor_tensor(KK[:, :, 48:64], KK[:, :, 48:64], b[:, :, 48:64], ALU.add), "K1")
            n = first["K1"]
            dve.wait_ge(bank_drained[n % NB], n // NB + 1)
            dve.sem_inc(sem("windows"), 1)
            for i in (0, 2, 4):
                b = filled(dve, "U", i)
                copy_signal(U[:, 8 * i:8 * i + 8, :], b.rearrange("p (g x) -> p g x", x=TC), "U", i, "U_ready")
            for kb in range(6):
                b = filled(dve, "loc", 2 * kb)
                n = first["loc"] + 2 * kb
                drained(loc_out(dve.tensor_copy, b, kb, 0), "loc", 2 * kb)
                dve.wait_ge(bank_drained[n % NB], n // NB + 1)
                dve.sem_inc(sem("loc_ready_dve"), 1)
            link(dve.memset(SL[:, :, 0, 0, :], 0.0))
            link(dve.memset(SL[:, :, 1, NC, :], 0.0))
            link(dve.tensor_copy(SL[:, :, 0, 0, 1::2], ist[:, :, 0:NP]))
            link(dve.tensor_copy(SL[:, :, 1, NC, 1::2], ist[:, :, NP:G]))
            dve.sem_inc(sem("init_ready"), 1)
            dve.wait_ge(sem("loc_ready_act"), 6)
            scan(dve, sem("scan_dve_chain"), [(0, 0, NP), (1, 0, SPLIT)])
            dve.sem_inc(sem("scan_dve"), 1)
            link(dve.tensor_copy(fs[:, :, 0:NP], SL[:, :, 0, NC, 0::2]))
            for j in range(2, 5):
                mod_rows(j, 1 if j == 4 else None)
            dve.wait_ge(sem("scan_pool"), 1)
            link(dve.tensor_copy(fs[:, :, NP:G], SL[:, :, 1, 0, 0::2]))
            dve.sem_inc(sem("fs_ready"), 1)
            dve.wait_ge(sem("du_ready"), 2)
            for kb in range(3):
                for g2 in range(2):
                    rows = slice(64 * g2, 64 * g2 + 64)
                    b = filled(dve, f"y{kb}", g2)
                    y = DU[rows, 8 * kb:8 * kb + 8, :]
                    drained(dve.tensor_tensor(y, y, b[rows, :].rearrange("p (k x) -> p k x", x=TC), ALU.add),
                            f"y{kb}", g2)
                    n = first[f"y{kb}"] + g2
                    dve.wait_ge(bank_drained[n % NB], n // NB + 1)
                    dve.sem_inc(sem("yb_ready"), 1)
            for i in (0, 2, 4):
                b = filled(dve, "zc", i)
                copy_signal(zc_view(i), b[0:64, :].rearrange("p (g j h) -> p g j h", j=CH, h=HS), "zc", i, "zc_ready")
            dve.wait_ge(sem("state_out"), 32)
            for i in (0, 2):
                b = filled(dve, "zT", i)
                copy_signal(zT[:, 2 * i:2 * i + 2, :], b.rearrange("p (t x) -> p t x", x=256), "zT", i, "zT_ready")
            for i in range(3):
                dve.wait_ge(sem("sg_ready"), i + 1)
                dve.wait_ge(sem("zT_ready"), 3)
                y = ycT[:, 2 * i:2 * i + 2, :]
                tt(y, y, zT[:, 2 * i:2 * i + 2, :], ALU.mult)
                dve.sem_inc(sem("yc_ready"), 1)
            dve.wait_ge(sem("g1_ready"), 4)
            for tau in range(2):
                for dh in range(2):
                    i = 2 * tau + dh
                    b = filled(dve, "o", i)
                    tt(otmp[:, :], b, g1s[:, dh * HALF:(dh + 1) * HALF], ALU.mult)
                    dve.sem_inc(bank_drained[(first["o"] + i) % NB], 1)
                    x = x_tok[:, tau, dh * HALF:(dh + 1) * HALF]
                    tt(x, x, otmp[:, :], ALU.add)
                    dve.sem_inc(sem("x2_ready"), 1)
            norm_scale(2)
            modulate(h2, "gs2", "sh2", "h2_ready")
            for i in (0, 2):
                b = filled(dve, "h2T", i)
                copy_signal(hT[:, 2 * i:2 * i + 2, :], b.rearrange("p (k x) -> p k x", x=256), "h2T", i, "h2T_ready")
            mod_rows(5)
            b = filled(dve, "lg")
            link(dve.tensor_copy(lg[:, :, :], b[:, 0:2 * NE].rearrange("p (t e) -> p t e", e=NE)))
            dve.sem_inc(bank_drained[first["lg"] % NB], 1)
            for tau in range(2):
                link(dve.max(m8[:, tau, :], lg[:, tau, :]))
            wide = lambda a: a.broadcast_to([P, 2, NE])
            fourth = wide(m8[:, :, 3:4])
            tt(eq[0][:, :, :], lg[:, :, :], wide(m8[:, :, 0:1]), ALU.subtract)
            dve.sem_inc(sem("lmax_ready"), 1)
            tt(gt[:, :, :], lg[:, :, :], fourth, ALU.is_gt)
            dve.wait_ge(sem("ex_ready"), 1)
            tt(rank[:, :, :], lg[:, :, :], fourth, ALU.is_equal)
            link(dve.tensor_copy(eq[0][:, :, :], rank[:, :, :]))
            a_, b_ = eq
            for sft in (1, 2, 4, 8, 16):
                dve.tensor_copy(b_[:, :, 0:sft], a_[:, :, 0:sft])
                tt(b_[:, :, sft:NE], a_[:, :, sft:NE], a_[:, :, 0:NE - sft], ALU.add)
                a_, b_ = b_, a_
            link(dve.tensor_reduce(r1c[:, 0:2], gt[:, :, :], AX.X, ALU.add))
            tt(a_[:, :, :], a_[:, :, :], wide(r1c[:, 0:2].unsqueeze(2)), ALU.add)
            link(dve.scalar_tensor_tensor(out=a_[:, :, :], in0=a_[:, :, :], scalar=4.0, in1=rank[:, :, :],
                                          op0=ALU.is_le, op1=ALU.mult))
            tt(gt[:, :, :], gt[:, :, :], a_[:, :, :], ALU.add)
            dve.sem_inc(sem("mask_ready"), 1)
            tt(ex[:, :, :], ex[:, :, :], gt[:, :, :], ALU.mult)
            link(dve.tensor_reduce(r1c[:, 4:6], ex[:, :, :], AX.X, ALU.add))
            link(dve.reciprocal(r1c[:, 6:8], r1c[:, 4:6]))
            tt(comb[:, :, :], ex[:, :, :], wide(r1c[:, 6:8].unsqueeze(2)), ALU.mult)
            dve.sem_inc(sem("comb_ready"), 1)
            b = filled(dve, "rk")
            link(dve.tensor_copy(cnt[:, 0:1], b[0:NE, 64:65]))
            link(dve.scalar_tensor_tensor(out=rank[:, :, :], in0=b[:, 0:2 * NE].rearrange("p (t e) -> p t e", e=NE),
                                          scalar=1.0, in1=gt[:, :, :], op0=ALU.add, op1=ALU.mult))
            dve.sem_inc(bank_drained[first["rk"] % NB], 1)
            link(dve.tensor_scalar(rank[:, :, :], rank[:, :, :], -1.0, None, ALU.add))
            link(dve.tensor_scalar(cnt[:, 1:2], cnt[:, 0:1], float(SL_), 1.0, ALU.is_gt, ALU.add))
            for n in range(2, 2 * L // SL_):
                link(dve.scalar_tensor_tensor(out=cnt[:, 1:2], in0=cnt[:, 0:1], scalar=float(n * SL_), in1=cnt[:, 1:2],
                                              op0=ALU.is_gt, op1=ALU.add))
            dve.sem_inc(sem("rounds_ready"), 1)
            b = filled(dve, "cu")
            tt(cnt[:, 4:5], b[0:NE, 0:1], cnt[:, 1:2], ALU.add)
            dve.sem_inc(bank_drained[first["cu"] % NB], 1)
            link(dve.tensor_scalar(cmp[:, 0:NRT], C("iota", slice(0, NE))[:, 0:NRT], cnt[:, 4:5], None, ALU.is_ge))
            dve.sem_inc(sem("cmp_ready"), 1)
            b = filled(dve, "tb")
            link(dve.tensor_scalar(tbl[:, 0:NRT], b[0:1, 0:NRT], float(NE - 1), None, ALU.min))
            tt(brt_f[:, 0:NRT], C("iota", slice(0, 1))[:, 0:NRT], b[0:1, NRT:2 * NRT], ALU.subtract)
            link(dve.tensor_scalar(tbl[:, NRT:2 * NRT], brt_f[:, 0:NRT], float(SL_), None, ALU.mult))
            link(dve.tensor_copy(tbl[:, 2 * NRT:2 * NRT + 1 + NE], b[0:1, 2 * NRT:2 * NRT + 1 + NE]))
            dve.sem_inc(bank_drained[first["tb"] % NB], 1)
            dve.sem_inc(sem("tables"), 1)
            b = filled(dve, "cb")
            link(dve.tensor_copy(combT[:, :], b[0:NE, 0:256]))
            dve.sem_inc(bank_drained[first["cb"] % NB], 1)
            dve.sem_inc(sem("combT_ready"), 1)
            total = dve.value_load(tbl[0:1, 2 * NRT + NE:2 * NRT + NE + 1], min_val=NE, max_val=NR)

            lo = _C["iota"][0]

            def expert_of(r):
                e = dve.value_load(tbl[0:1, bass.ds(r, 1)], min_val=0, max_val=NE - 1)
                base = dve.value_load(tbl[0:1, bass.ds(r + NRT, 1)], min_val=0, max_val=256 - SL_)
                return e, cst[:, bass.ds(base + lo, SL_)]

            def select(r):
                e, slots = expert_of(r)
                for tau in range(2):
                    ins = dve.tensor_scalar(sel[:, tau, :], slots, rank[:, tau, bass.ds(e, 1)], None, ALU.is_equal)
                ins.then_inc(sem("sel_ready"), 1)
                return e

            def select_weighted(r):
                e, slots = expert_of(r)
                for tau in range(2):
                    for n in range(2):
                        ins = dve.tensor_scalar(selw[:, tau, n, :], slots, rank[:, tau, bass.ds(e, 1)],
                                                comb[:, tau, bass.ds(e, 1)], ALU.is_equal, ALU.mult)
                ins.then_inc(sem("selw_ready"), 1)

            def bias_row(e):
                dve.tensor_copy(selb[:, :], cst[0:96, bass.ds(e + _C["eye"][0], 1)].broadcast_to([96, SL_]))\
                    .then_inc(sem("selb_ready"), 1)

            bias_row(select(0))
            dve.memset(ys[:, :], 0.0).then_inc(sem("ys_ready"), 1)
            dve.wait_ge(sem("combT_used"), 1)
            dve.memset(selT[:, :], 0.0).then_inc(sem("selT_ready"), 1)
            dve.wait_ge(sem("X_turned"), 1)
            dve.tensor_copy(XT[:, :, :], pT.rearrange("p (n x) -> p n x", x=P)).then_inc(sem("XT_ready"), 1)
            with dve.Fori(0, total) as R:
                dve.wait_ge(sem("gathered"), R + 1)
                e1 = select(R + 1)
                select_weighted(R)
                dve.wait_ge(unit_used[1], R + 1)
                dve.tensor_scalar(gcl[:, :], pG, 7.0, None, ALU.min).then_inc(sem("gcl_ready"), 1)
                dve.wait_ge(unit_used[3], R + 1)
                dve.tensor_scalar(upc[:, :], pU, 7.0, -7.0, ALU.min, ALU.max).then_inc(sem("upc_ready"), 1)
                dve.wait_ge(sem("upc_ready"), R + 1)
                dve.wait_ge(sem("gcl_ready"), R + 1)
                dve.scalar_tensor_tensor(out=upc[:, :], in0=upc[:, :], scalar=1.0, in1=gcl[:, :], op0=ALU.add,
                                         op1=ALU.mult).then_inc(sem("glin_ready"), 1)
                bias_row(e1)
                dve.wait_ge(sem("glin_ready"), R + 1)
                dve.wait_ge(sem("sgm_ready"), R + 1)
                dve.tensor_tensor(acts[:, :], upc[:, :], sgm[:, :], ALU.mult).then_inc(sem("act_ready"), 1)
                dve.wait_ge(sem("act_turned"), R + 1)
                dve.tensor_copy(actT[:, :, :], pG.rearrange("p (n x) -> p n x", x=P)).then_inc(sem("actT_ready"), 1)
                dve.wait_ge(sem("X_turned"), R + 2)
                dve.tensor_copy(XT[:, :, :], pT.rearrange("p (n x) -> p n x", x=P)).then_inc(sem("XT_ready"), 1)
                dve.wait_ge(sem("sel_turned"), R + 1)
            dve.wait_ge(sem("scattered"), total + 1)
            dve.wait_ge(sem("g2_ready"), 4)
            for tau in range(2):
                for dh in range(2):
                    tt(Xs[:, :], OUT[tau][dh], g2s[:, dh * HALF:(dh + 1) * HALF], ALU.mult)
                    x = x_tok[:, tau, dh * HALF:(dh + 1) * HALF]
                    tt(x, x, Xs[:, :], ALU.add)
                    dve.sem_inc(sem("x3_ready"), 1)
            norm_scale(3)
            dve.wait_ge(sem("gainf_ready"), 4)
            for tau in range(2):
                link(dve.scalar_tensor_tensor(out=h2[:, tau, :], in0=x_tok[:, tau, :], scalar=ss[:, 6 + tau:7 + tau],
                                              in1=gfs[:, :], op0=ALU.mult, op1=ALU.mult))
                dve.sem_inc(sem("y_ready"), 1)


_INS = ['x_prompt', 'x_sample', 'c', 'state_s5_re', 'state_s5_im', 'c_ctx', 'w_ada', 'b_ada', 'norm1_g', 'w_in',
        's5_lam_re', 's5_lam_im', 's5_log_dt', 's5_b_re', 's5_b_im', 's5_c_re', 's5_c_im', 's5_d', 's5_w_glu',
        'w_fnet', 'w_out', 'norm2_g', 'w_router', 'b_router', 'w_gate', 'b_gate', 'w_up', 'b_up', 'w_down',
        'b_down', 'norm_f_g']
_OUTS = [(1, L, D), (1, L, D), (1, 1, 2, G, ST), (1, 1, 2, G, ST)]


def kernel(**inputs):
    import concourse.bacc as bacc
    from concourse.bass_utils import run_bass_kernel_spmd

    nc = bacc.Bacc("TRN2", target_bir_lowering=False, num_devices=1)
    arrays, args = {}, []
    for name, a in [("constants", constant_tile()), ("positions", position_table())] + \
            [(n, inputs[n]) for n in _INS]:
        a = np.ascontiguousarray(a)
        arrays[f"in_{name}"] = a
        args.append(nc.dram_tensor(f"in_{name}", a.shape, mybir.dt.from_np(a.dtype), kind="ExternalInput").ap())
    for i, shape in enumerate(_OUTS):
        args.append(nc.dram_tensor(f"out_{i}", shape, F32, kind="ExternalOutput").ap())
    build(nc, *args)
    r = run_bass_kernel_spmd(nc, [arrays], core_ids=[0])
    return tuple(r.results[0][f"out_{i}"] for i in range(len(_OUTS)))
```
